# Optimizing a Trainium2 kernel written in Bass

```python
import math
import jax
import jax.numpy as jnp
from jax import lax
import numpy as np
import jax, jax.numpy as jnp

D_MODEL = 1024
BATCH = 1
SEQ = 512
DEPTH = 2

GRID_W = 64
CTX_LEN = 256
HEAD_DIM = 64
MIX_HEADS = D_MODEL // HEAD_DIM
A_Q_HEADS = MIX_HEADS // 2
A_KV_HEADS = A_Q_HEADS // 4
B_Q_HEADS = MIX_HEADS - A_Q_HEADS
B_KV_HEADS = B_Q_HEADS // 4
WINDOW = 128
BLOCK = 128
NA_ROWS = 8
NA_COLS = 16
NA_QCOLS = 16
NA_KCOLS = NA_QCOLS + NA_COLS
C_HEADS = D_MODEL // (2 * HEAD_DIM)
C_V_DIM = 2 * HEAD_DIM
D_FF = 4 * D_MODEL
ROPE_THETA = 10000.0
EPS = 1e-6

A_QW = A_Q_HEADS * HEAD_DIM
A_KVW = A_KV_HEADS * HEAD_DIM
B_QW = B_Q_HEADS * HEAD_DIM
B_KVW = B_KV_HEADS * HEAD_DIM
EVEN_WIDTHS = (A_QW, A_KVW, A_KVW, B_QW, B_KVW, B_KVW)
EVEN_IN = A_QW + 2 * A_KVW + B_QW + 2 * B_KVW
EVEN_OUT = A_QW + B_QW
C_QKW = C_HEADS * 2 * HEAD_DIM
C_VW = C_HEADS * C_V_DIM
ODD_IN = 2 * C_QKW + C_VW


def _rms_norm(x, g):
    xf = x.astype(jnp.float32)
    y = xf * lax.rsqrt(jnp.mean(xf * xf, axis=-1, keepdims=True) + EPS)
    return (y * g.astype(jnp.float32)).astype(x.dtype)

def _modulate(x, g, shift, scale):
    return _rms_norm(x, g) * (1 + scale) + shift

def _rope_tables(n):
    t = jnp.arange(n, dtype=jnp.int32)
    row = (t // GRID_W).astype(jnp.float32)
    col = (t % GRID_W).astype(jnp.float32)
    quarter = HEAD_DIM // 4
    inv_freq = ROPE_THETA ** (-jnp.arange(quarter, dtype=jnp.float32) / quarter)
    ar = row[:, None] * inv_freq[None, :]
    ac = col[:, None] * inv_freq[None, :]
    ang = jnp.concatenate([ar, ar, ac, ac], axis=-1)
    return jnp.cos(ang), jnp.sin(ang)

def _apply_rope(x, cos, sin):
    xs = x.reshape(x.shape[:-1] + (2, 2, HEAD_DIM // 4))
    rot = jnp.stack([-xs[..., 1, :], xs[..., 0, :]], axis=-2).reshape(x.shape)
    return x * cos[:, None, :].astype(x.dtype) + rot * sin[:, None, :].astype(x.dtype)

def _ctx_attn(q, k, v, sink):
    b, n, hq, d = q.shape
    hkv = k.shape[2]
    g = hq // hkv
    qg = q.reshape(b, n, hkv, g, d)
    s = jnp.einsum('bqhgd,bkhd->bhgqk', qg, k).astype(jnp.float32) * d ** -0.5
    if sink is not None:
        sk = jnp.broadcast_to(sink.astype(jnp.float32).reshape(1, hkv, g, 1, 1), s.shape[:-1] + (1,))
        s = jnp.concatenate([s, sk], axis=-1)
    p = jax.nn.softmax(s, axis=-1)[..., :n].astype(v.dtype)
    return jnp.einsum('bhgqk,bkhd->bqhgd', p, v).reshape(b, n, hq * d)

def _window_attn(q, k, v, kc, vc, sink):
    b, n, hq, d = q.shape
    hkv = k.shape[2]
    g = hq // hkv
    nb = n // BLOCK
    qb = q.reshape(b, nb, BLOCK, hkv, g, d)
    pad = ((0, 0), (BLOCK, BLOCK), (0, 0), (0, 0))

    def band(t):
        tp = jnp.pad(t, pad).reshape(b, nb + 2, BLOCK, hkv, d)
        return jnp.concatenate([tp[:, :-2], tp[:, 1:-1], tp[:, 2:]], axis=2)

    kb, vb = band(k), band(v)
    scale = d ** -0.5
    s_lat = jnp.einsum('bnqhgd,bnkhd->bhgnqk', qb, kb).astype(jnp.float32) * scale
    blk = jnp.arange(nb)[:, None, None] * BLOCK
    qpos = blk + jnp.arange(BLOCK)[None, :, None]
    kpos = blk - BLOCK + jnp.arange(3 * BLOCK)[None, None, :]
    valid = (jnp.abs(qpos - kpos) <= WINDOW) & (kpos >= 0) & (kpos < n)
    s_lat = jnp.where(valid, s_lat, -jnp.inf)
    s_ctx = jnp.einsum('bnqhgd,bchd->bhgnqc', qb, kc).astype(jnp.float32) * scale
    s_sink = jnp.broadcast_to(sink.astype(jnp.float32).reshape(1, hkv, g, 1, 1, 1), s_ctx.shape[:-1] + (1,))
    p = jax.nn.softmax(jnp.concatenate([s_lat, s_ctx, s_sink], axis=-1), axis=-1).astype(v.dtype)
    nk, nc = 3 * BLOCK, kc.shape[1]
    out = (jnp.einsum('bhgnqk,bnkhd->bnqhgd', p[..., :nk], vb)
           + jnp.einsum('bhgnqc,bchd->bnqhgd', p[..., nk:nk + nc], vc))
    return out.reshape(b, n, hq * d)

def _neighbourhood_attn(q, k, v, kc, vc, rpb):
    b, n, hq, d = q.shape
    hkv = k.shape[2]
    g = hq // hkv
    rows = n // GRID_W
    kr = min(NA_ROWS, rows)
    ncb = GRID_W // NA_QCOLS
    nkey = kr * NA_KCOLS
    r = jnp.arange(rows)
    row_idx = jnp.clip(r - kr // 2, 0, rows - kr)[:, None] + jnp.arange(kr)[None, :]
    m = jnp.arange(ncb)
    col_idx = jnp.clip(m * NA_QCOLS - NA_COLS // 2, 0, GRID_W - NA_KCOLS)[:, None] + jnp.arange(NA_KCOLS)[None, :]
    qcol = m[:, None] * NA_QCOLS + jnp.arange(NA_QCOLS)[None, :]
    cstart = jnp.clip(qcol - NA_COLS // 2, 0, GRID_W - NA_COLS)
    kcol = col_idx[:, None, :]
    col_ok = (kcol >= cstart[..., None]) & (kcol < cstart[..., None] + NA_COLS)
    mask = jnp.broadcast_to(col_ok[:, :, None, :], (ncb, NA_QCOLS, kr, NA_KCOLS)).reshape(ncb, NA_QCOLS, nkey)

    def gather(t):
        tg = t.reshape(b, rows, GRID_W, hkv, d)
        tb = tg[:, row_idx[:, None, :, None], col_idx[None, :, None, :]]
        return tb.reshape(b, rows, ncb, nkey, hkv, d)

    kb, vb = gather(k), gather(v)
    roff = row_idx - r[:, None] + (NA_ROWS - 1)
    coff = jnp.clip(kcol - qcol[..., None], 1 - NA_COLS, NA_COLS - 1) + (NA_COLS - 1)
    bias = rpb[:, roff[:, :, None, None, None], coff[None, None]]
    bias = jnp.transpose(bias, (0, 1, 3, 4, 2, 5)).reshape(hkv, g, rows, ncb, NA_QCOLS, nkey).astype(jnp.float32)
    qb = q.reshape(b, rows, ncb, NA_QCOLS, hkv, g, d)
    scale = d ** -0.5
    s_nb = jnp.einsum('brmqhgd,brmkhd->bhgrmqk', qb, kb).astype(jnp.float32) * scale + bias
    s_nb = jnp.where(mask, s_nb, -jnp.inf)
    s_ctx = jnp.einsum('brmqhgd,bchd->bhgrmqc', qb, kc).astype(jnp.float32) * scale
    p = jax.nn.softmax(jnp.concatenate([s_nb, s_ctx], axis=-1), axis=-1).astype(v.dtype)
    out = (jnp.einsum('bhgrmqk,brmkhd->brmqhgd', p[..., :nkey], vb)
           + jnp.einsum('bhgrmqc,bchd->brmqhgd', p[..., nkey:], vc))
    return out.reshape(b, n, hq * d)

def _split_even(p):
    b, n, _ = p.shape
    idx = np.cumsum(EVEN_WIDTHS)[:-1].tolist()
    parts = jnp.split(p, idx, axis=-1)
    return [t.reshape(b, n, -1, HEAD_DIM) for t in parts]

def _even_mixer(hx, hc, w_in, w_out, sink, rpb, cos, sin, with_ctx):
    aq, ak, av, bq, bk, bv = _split_even(hx @ w_in)
    caq, cak, cav, cbq, cbk, cbv = _split_even(hc @ w_in)
    aq = _apply_rope(aq, cos, sin)
    ak = _apply_rope(ak, cos, sin)
    ya = _window_attn(aq, ak, av, cak, cav, sink)
    yb = _neighbourhood_attn(bq, bk, bv, cbk, cbv, rpb)
    y_x = jnp.concatenate([ya, yb], axis=-1) @ w_out
    if not with_ctx:
        return y_x, None
    y_c = jnp.concatenate([_ctx_attn(caq, cak, cav, sink), _ctx_attn(cbq, cbk, cbv, None)], axis=-1) @ w_out
    return y_x, y_c

def _split_odd(p):
    b, n, _ = p.shape
    q, k, v = jnp.split(p, [C_QKW, 2 * C_QKW], axis=-1)
    return (q.reshape(b, n, C_HEADS, 2, HEAD_DIM), k.reshape(b, n, C_HEADS, 2, HEAD_DIM),
            v.reshape(b, n, C_HEADS, C_V_DIM))

def _diff_core(q, k, v, lam, sub_g, lam_init):
    b, nq, h, _, d = q.shape
    s = jnp.einsum('bqhmd,bkhmd->bhmqk', q, k).astype(jnp.float32) * d ** -0.5
    p = jax.nn.softmax(s, axis=-1)
    a = (p[:, :, 0] - lam * p[:, :, 1]).astype(v.dtype)
    o = jnp.einsum('bhqk,bkhe->bqhe', a, v)
    o = _rms_norm(o, sub_g) * (1.0 - lam_init)
    return o.reshape(b, nq, h * v.shape[-1])

def _odd_mixer(hx, hc, w_in, w_out, lq1, lk1, lq2, lk2, sub_g, lam_init, cos, sin, with_ctx):
    q, k, v = _split_odd(hx @ w_in)
    cq, ck, cv = _split_odd(hc @ w_in)
    b, n = q.shape[:2]
    q = _apply_rope(q.reshape(b, n, 2 * C_HEADS, HEAD_DIM), cos, sin).reshape(q.shape)
    k = _apply_rope(k.reshape(b, n, 2 * C_HEADS, HEAD_DIM), cos, sin).reshape(k.shape)
    f32 = jnp.float32
    lam = (jnp.exp(jnp.sum(lq1.astype(f32) * lk1.astype(f32)))
           - jnp.exp(jnp.sum(lq2.astype(f32) * lk2.astype(f32))) + lam_init)
    kf = jnp.concatenate([k, ck], axis=1)
    vf = jnp.concatenate([v, cv], axis=1)
    nb = n // BLOCK
    qb = jnp.swapaxes(q.reshape(b, nb, BLOCK, C_HEADS, 2, HEAD_DIM), 0, 1)
    yx = lax.map(lambda qblk: _diff_core(qblk, kf, vf, lam, sub_g, lam_init), qb)
    yx = jnp.swapaxes(yx, 0, 1).reshape(b, n, C_VW) @ w_out
    if not with_ctx:
        return yx, None
    yc = _diff_core(cq, ck, cv, lam, sub_g, lam_init) @ w_out
    return yx, yc

def _mlp(h, w1, w2):
    a = jax.nn.relu(h @ w1)
    return (a * a) @ w2

def first_inputs(seed: int = 0) -> dict:
    key = jax.random.key(seed)
    ks = jax.random.split(key, 22)
    n_even = (DEPTH + 1) // 2
    n_odd = DEPTH // 2

    def nrm(k, shape, s):
        return jax.random.normal(k, shape, jnp.float32) * s

    return {
        'x': nrm(ks[0], (BATCH, SEQ, D_MODEL), 1.0),
        'c': nrm(ks[1], (BATCH, D_MODEL), 1.0),
        'ctx': nrm(ks[2], (BATCH, CTX_LEN, D_MODEL), 1.0),
        'c_ctx': nrm(ks[3], (D_MODEL,), 1.0),
        'ada_w': nrm(ks[4], (DEPTH, D_MODEL, 6 * D_MODEL), 0.5 * D_MODEL ** -0.5),
        'ada_b': nrm(ks[5], (DEPTH, 6 * D_MODEL), 0.01),
        'norm1_g': 1.0 + nrm(ks[6], (DEPTH, D_MODEL), 0.05),
        'norm2_g': 1.0 + nrm(ks[7], (DEPTH, D_MODEL), 0.05),
        'even_w_in': nrm(ks[8], (n_even, D_MODEL, EVEN_IN), D_MODEL ** -0.5),
        'even_w_out': nrm(ks[9], (n_even, EVEN_OUT, D_MODEL), EVEN_OUT ** -0.5),
        'a_sink': nrm(ks[10], (n_even, A_Q_HEADS), 0.5),
        'b_rpb': nrm(ks[11], (n_even, B_Q_HEADS, 2 * NA_ROWS - 1, 2 * NA_COLS - 1), 0.1),
        'odd_w_in': nrm(ks[12], (n_odd, D_MODEL, ODD_IN), D_MODEL ** -0.5),
        'odd_w_out': nrm(ks[13], (n_odd, C_VW, D_MODEL), C_VW ** -0.5),
        'lam_q1': nrm(ks[14], (n_odd, HEAD_DIM), 0.1),
        'lam_k1': nrm(ks[15], (n_odd, HEAD_DIM), 0.1),
        'lam_q2': nrm(ks[16], (n_odd, HEAD_DIM), 0.1),
        'lam_k2': nrm(ks[17], (n_odd, HEAD_DIM), 0.1),
        'subln_g': 1.0 + nrm(ks[18], (n_odd, C_V_DIM), 0.05),
        'mlp_w1': nrm(ks[19], (DEPTH, D_MODEL, D_FF), D_MODEL ** -0.5),
        'mlp_w2': nrm(ks[20], (DEPTH, D_FF, D_MODEL), D_FF ** -0.5),
        'final_g': 1.0 + nrm(ks[21], (D_MODEL,), 0.05),
    }

def first_block(x, c, ctx, c_ctx, ada_w, ada_b, norm1_g, norm2_g, even_w_in, even_w_out, a_sink, b_rpb,
              odd_w_in, odd_w_out, lam_q1, lam_k1, lam_q2, lam_k2, subln_g, mlp_w1, mlp_w2, final_g):
    n = x.shape[1]
    cos, sin = _rope_tables(n)
    hx, hc = x, ctx
    for i in range(DEPTH):
        with_ctx = i < DEPTH - 1
        j = i // 2
        mx = (jax.nn.silu(c) @ ada_w[i] + ada_b[i])[:, None, :]
        mc = jax.nn.silu(c_ctx) @ ada_w[i] + ada_b[i]
        sx1, cx1, gx1, sx2, cx2, gx2 = jnp.split(mx, 6, axis=-1)
        sc1, cc1, gc1, sc2, cc2, gc2 = jnp.split(mc, 6, axis=-1)
        ax = _modulate(hx, norm1_g[i], sx1, cx1)
        ac = _modulate(hc, norm1_g[i], sc1, cc1)
        if i % 2 == 0:
            yx, yc = _even_mixer(ax, ac, even_w_in[j], even_w_out[j], a_sink[j], b_rpb[j], cos, sin, with_ctx)
        else:
            lam_init = 0.8 - 0.6 * math.exp(-0.3 * i)
            yx, yc = _odd_mixer(ax, ac, odd_w_in[j], odd_w_out[j], lam_q1[j], lam_k1[j], lam_q2[j], lam_k2[j],
                                subln_g[j], lam_init, cos, sin, with_ctx)
        hx = hx + gx1 * yx
        hx = hx + gx2 * _mlp(_modulate(hx, norm2_g[i], sx2, cx2), mlp_w1[i], mlp_w2[i])
        if with_ctx:
            hc = hc + gc1 * yc
            hc = hc + gc2 * _mlp(_modulate(hc, norm2_g[i], sc2, cc2), mlp_w1[i], mlp_w2[i])
    return _rms_norm(hx, final_g)


CONV_CH = D_MODEL // 4
CONV_WIDTH = 31
ATT_WIDTH = 3 * D_MODEL // 8
N_ATT_HEADS = ATT_WIDTH // HEAD_DIM
DILATION_PAIRS = ((128, 1), (512, 4), (2048, 16))
ATT_BLOCK = 128
ALIBI_MAX_EXP = 8.0
MASK_VALUE = -1e30
REC_WIDTH = 3 * D_MODEL // 8
REC_KEY_DIM = 64
REC_VAL_DIM = 64
N_REC_HEADS = REC_WIDTH // REC_VAL_DIM
REC_KEY_WIDTH = N_REC_HEADS * REC_KEY_DIM
REC_CHUNK = 64
F_TINY = 1e-30
MIX_WIDTH = CONV_CH + ATT_WIDTH + REC_WIDTH
IN_SPLITS = (CONV_CH, CONV_CH, ATT_WIDTH, ATT_WIDTH, ATT_WIDTH,
             REC_KEY_WIDTH, REC_KEY_WIDTH, REC_KEY_WIDTH, REC_WIDTH, REC_WIDTH)
IN_COLS = sum(IN_SPLITS)
D_FF_2 = ((8 * D_MODEL // 3 + 127) // 128) * 128
FFN_CONV_WIDTH = 3
N_MOD = 6


def _rmsnorm(x, w):
    xf = x.astype(jnp.float32)
    y = xf * lax.rsqrt(jnp.mean(xf * xf, axis=-1, keepdims=True) + EPS)
    return (y * w.astype(jnp.float32)).astype(x.dtype)

def _layernorm(x, w, b):
    xf = x.astype(jnp.float32)
    mu = jnp.mean(xf, axis=-1, keepdims=True)
    var = jnp.mean(jnp.square(xf - mu), axis=-1, keepdims=True)
    y = (xf - mu) * lax.rsqrt(var + EPS)
    return (y * w.astype(jnp.float32) + b.astype(jnp.float32)).astype(x.dtype)

def _depthwise_conv(x, w, b=None):
    k_w, ch = w.shape
    y = lax.conv_general_dilated(
        x, w[:, None, :].astype(x.dtype), window_strides=(1,),
        padding=[(k_w // 2, k_w // 2)],
        dimension_numbers=('NWC', 'WIO', 'NWC'), feature_group_count=ch)
    if b is not None:
        y = y + b.astype(x.dtype)
    return y

def _dilated_window_attention(q, k, v, slopes, window, dilation):
    B, S, H, Dh = q.shape
    half = window // (2 * dilation)
    L = S // dilation

    def to_sub(t):
        return t.reshape(B, L, dilation, H, Dh).transpose(0, 2, 1, 3, 4).reshape(B * dilation, L, H, Dh)

    qs, ks, vs = to_sub(q), to_sub(k), to_sub(v)
    blk = min(ATT_BLOCK, L)
    nb = -(-L // blk)
    Lp = nb * blk
    span = blk + 2 * half
    qs = jnp.pad(qs, ((0, 0), (0, Lp - L), (0, 0), (0, 0)))
    pad_k = ((0, 0), (half, half + Lp - L), (0, 0), (0, 0))
    ks = jnp.pad(ks, pad_k)
    vs = jnp.pad(vs, pad_k)
    idx = (np.arange(nb) * blk)[:, None] + np.arange(span)[None, :]
    kb = ks[:, idx]
    vb = vs[:, idx]
    qb = qs.reshape(B * dilation, nb, blk, H, Dh)
    rel = np.arange(span)[None, :] - half - np.arange(blk)[:, None]
    key_pos = idx - half
    valid = ((np.abs(rel) <= half)[None]
             & (key_pos[:, None, :] >= 0) & (key_pos[:, None, :] < L))
    dist = jnp.asarray(np.abs(rel) * dilation, jnp.float32)
    scores = jnp.einsum('bnqhd,bnkhd->bnhqk', qb, kb) * (Dh ** -0.5)
    scores = scores - slopes[:, None, None] * dist
    scores = jnp.where(jnp.asarray(valid)[:, None], scores, MASK_VALUE)
    lse = jax.nn.logsumexp(scores, axis=-1)
    p = jnp.exp(scores - lse[..., None])
    o = jnp.einsum('bnhqk,bnkhd->bnqhd', p, vb).reshape(B * dilation, Lp, H, Dh)[:, :L]
    lse = lse.transpose(0, 1, 3, 2).reshape(B * dilation, Lp, H)[:, :L]

    def from_sub(t):
        t5 = t.reshape((B, dilation, L) + t.shape[2:])
        t5 = jnp.moveaxis(t5, 1, 2)
        return t5.reshape((B, S) + t5.shape[3:])

    return from_sub(o), from_sub(lse)

def _mixture_of_dilated_attention(q, k, v):
    slopes = jnp.asarray(2.0 ** (-ALIBI_MAX_EXP * np.arange(1, N_ATT_HEADS + 1) / N_ATT_HEADS), jnp.float32)
    outs, lses = [], []
    for window, dilation in DILATION_PAIRS:
        o_g, l_g = _dilated_window_attention(q, k, v, slopes, window, dilation)
        outs.append(o_g)
        lses.append(l_g)
    wts = jax.nn.softmax(jnp.stack(lses, 0), axis=0)
    return jnp.einsum('gbsh,gbshd->bshd', wts, jnp.stack(outs, 0))

def _hgrn2_scan(q, k, v, logf):
    B, S, H, dk = q.shape
    dv = v.shape[-1]
    n = S // REC_CHUNK

    def chunks(t):
        return t.reshape(B, n, REC_CHUNK, H, t.shape[-1]).transpose(1, 0, 3, 2, 4)

    qc, kc, vc = chunks(q), chunks(k), chunks(v)
    bc = jnp.cumsum(chunks(logf), axis=3)
    lower = jnp.asarray(np.tril(np.ones((REC_CHUNK, REC_CHUNK), bool)))[:, :, None]

    def step(state, inp):
        qt, kt, vt, bt = inp
        diff = bt[:, :, :, None, :] - bt[:, :, None, :, :]
        decay = jnp.where(lower, jnp.exp(jnp.where(lower, diff, 0.0)), 0.0)
        scores = jnp.einsum('bhtk,bhsk,bhtsk->bhts', qt, kt, decay)
        o = (jnp.einsum('bhts,bhsv->bhtv', scores, vt)
             + jnp.einsum('bhtk,bhkv->bhtv', qt * jnp.exp(bt), state))
        b_last = bt[:, :, -1:, :]
        state = (jnp.exp(b_last[:, :, 0, :])[..., None] * state
                 + jnp.einsum('bhsk,bhsv->bhkv', kt * jnp.exp(b_last - bt), vt))
        return state, o

    state0 = jnp.zeros((B, H, dk, dv), q.dtype)
    _, o = lax.scan(step, state0, (qc, kc, vc, bc))
    return o.transpose(1, 0, 3, 2, 4).reshape(B, S, H, dv)

def _hgrn2_gate(z, lb):
    f = lb + (1.0 - lb) * jax.nn.sigmoid(z)
    logf = jnp.log(jnp.maximum(f, F_TINY))
    k = (1.0 - lb) * jax.nn.sigmoid(-z)
    return logf, k

def _token_mixers(h, w_in, conv_w, conv_b, ln_w, ln_b, lb_fwd, lb_bwd, rec_norm_w, w_out):
    B, S, _ = h.shape
    f32 = jnp.float32
    proj = h @ w_in.astype(h.dtype)
    cuts = [int(c) for c in np.cumsum(IN_SPLITS)[:-1]]
    (a_val, a_gate, q_att, k_att, v_att,
     q_rec, z_fwd, z_bwd, i_rec, g_rec) = jnp.split(proj, cuts, axis=-1)

    a = a_val * jax.nn.sigmoid(a_gate)
    a = _depthwise_conv(a, conv_w, conv_b)
    a = jax.nn.silu(_layernorm(a, ln_w, ln_b))

    def heads(t, d):
        return t.astype(f32).reshape(B, S, -1, d)
    att = _mixture_of_dilated_attention(heads(q_att, HEAD_DIM), heads(k_att, HEAD_DIM), heads(v_att, HEAD_DIM))
    att = att.reshape(B, S, ATT_WIDTH).astype(h.dtype)

    qr = heads(jax.nn.silu(q_rec.astype(f32)), REC_KEY_DIM)
    vr = heads(i_rec, REC_VAL_DIM)
    logf_f, k_f = _hgrn2_gate(z_fwd.astype(f32), lb_fwd)
    logf_b, k_b = _hgrn2_gate(z_bwd.astype(f32), lb_bwd)
    o_f = _hgrn2_scan(qr, heads(k_f, REC_KEY_DIM), vr, heads(logf_f, REC_KEY_DIM))
    flip = lambda t: jnp.flip(t, axis=1)
    o_b = flip(_hgrn2_scan(flip(qr), flip(heads(k_b, REC_KEY_DIM)), flip(vr), flip(heads(logf_b, REC_KEY_DIM))))
    o_r = o_f + o_b
    o_r = o_r * lax.rsqrt(jnp.mean(o_r * o_r, axis=-1, keepdims=True) + EPS)
    o_r = o_r.reshape(B, S, REC_WIDTH) * rec_norm_w.astype(f32)
    rec = (o_r * jax.nn.silu(g_rec.astype(f32))).astype(h.dtype)

    mixed = jnp.concatenate([a, att, rec], axis=-1)
    return mixed @ w_out.astype(h.dtype)

def _conv_ffn(h, w_up, conv_w, w_down):
    u = h @ w_up.astype(h.dtype)
    u = _depthwise_conv(u, conv_w)
    gate, val = jnp.split(u, 2, axis=-1)
    return (jax.nn.gelu(gate, approximate=False) * val) @ w_down.astype(h.dtype)

def second_inputs(seed: int = 0) -> dict:
    key = jax.random.key(seed)
    ks = jax.random.split(key, 18)
    f32 = jnp.float32
    D = D_MODEL

    def nrm(k, shape, scale):
        return jax.random.normal(k, shape, f32) * scale

    return {
        "x": nrm(ks[0], (BATCH, SEQ, D), 1.0),
        "c": nrm(ks[1], (BATCH, D), 1.0),
        "w_ada": nrm(ks[2], (DEPTH, D, N_MOD * D), 0.5 * D ** -0.5),
        "b_ada": nrm(ks[3], (DEPTH, N_MOD * D), 0.02),
        "norm1_w": 1.0 + nrm(ks[4], (DEPTH, D), 0.05),
        "w_in": nrm(ks[5], (DEPTH, D, IN_COLS), D ** -0.5),
        "conv_a_w": nrm(ks[6], (DEPTH, CONV_WIDTH, CONV_CH), CONV_WIDTH ** -0.5),
        "conv_a_b": nrm(ks[7], (DEPTH, CONV_CH), 0.02),
        "ln_a_w": 1.0 + nrm(ks[8], (DEPTH, CONV_CH), 0.05),
        "ln_a_b": nrm(ks[9], (DEPTH, CONV_CH), 0.02),
        "lb_gamma": nrm(ks[10], (DEPTH, 2, REC_KEY_WIDTH), 1.0),
        "rec_norm_w": 1.0 + nrm(ks[11], (DEPTH, REC_WIDTH), 0.05),
        "w_out": nrm(ks[12], (DEPTH, MIX_WIDTH, D), MIX_WIDTH ** -0.5),
        "norm2_w": 1.0 + nrm(ks[13], (DEPTH, D), 0.05),
        "w_up": nrm(ks[14], (DEPTH, D, 2 * D_FF_2), D ** -0.5),
        "conv_f_w": nrm(ks[15], (DEPTH, FFN_CONV_WIDTH, 2 * D_FF_2), FFN_CONV_WIDTH ** -0.5),
        "w_down": nrm(ks[16], (DEPTH, D_FF_2, D), D_FF_2 ** -0.5),
        "final_norm_w": 1.0 + nrm(ks[17], (D,), 0.05),
    }

def second_block(x, c, w_ada, b_ada, norm1_w, w_in, conv_a_w, conv_a_b, ln_a_w, ln_a_b,
              lb_gamma, rec_norm_w, w_out, norm2_w, w_up, conv_f_w, w_down, final_norm_w):
    p = jax.nn.softmax(lb_gamma.astype(jnp.float32), axis=0)
    lower_bounds = jnp.cumsum(p, axis=0) - p[0:1]
    cond = jax.nn.silu(c)
    for l in range(DEPTH):
        mod = (cond @ w_ada[l] + b_ada[l]).astype(x.dtype)[:, None, :]
        sh1, sc1, g1, sh2, sc2, g2 = jnp.split(mod, N_MOD, axis=-1)
        h = _rmsnorm(x, norm1_w[l]) * (1.0 + sc1) + sh1
        x = x + g1 * _token_mixers(h, w_in[l], conv_a_w[l], conv_a_b[l], ln_a_w[l], ln_a_b[l],
                                   lower_bounds[l, 0], lower_bounds[l, 1], rec_norm_w[l], w_out[l])
        h = _rmsnorm(x, norm2_w[l]) * (1.0 + sc2) + sh2
        x = x + g2 * _conv_ffn(h, w_up[l], conv_f_w[l], w_down[l])
    return _rmsnorm(x, final_norm_w)


def setup_inputs(seed=0):
    out = dict(first_inputs(seed))
    for name, value in second_inputs(seed + 1).items():
        if name != "x":
            out[name + "_2"] = value
    return out


def reference(
    x, c, ctx, c_ctx, ada_w, ada_b, norm1_g, norm2_g, even_w_in, even_w_out, a_sink, b_rpb,
    odd_w_in, odd_w_out, lam_q1, lam_k1, lam_q2, lam_k2, subln_g, mlp_w1, mlp_w2, final_g, c_2,
    w_ada_2, b_ada_2, norm1_w_2, w_in_2, conv_a_w_2, conv_a_b_2, ln_a_w_2, ln_a_b_2, lb_gamma_2,
    rec_norm_w_2, w_out_2, norm2_w_2, w_up_2, conv_f_w_2, w_down_2, final_norm_w_2,
):
    x = first_block(
        x, c, ctx, c_ctx, ada_w, ada_b, norm1_g, norm2_g, even_w_in, even_w_out, a_sink, b_rpb,
        odd_w_in, odd_w_out, lam_q1, lam_k1, lam_q2, lam_k2, subln_g, mlp_w1, mlp_w2, final_g,
    )
    return second_block(
        x, c_2, w_ada_2, b_ada_2, norm1_w_2, w_in_2, conv_a_w_2, conv_a_b_2, ln_a_w_2, ln_a_b_2,
        lb_gamma_2, rec_norm_w_2, w_out_2, norm2_w_2, w_up_2, conv_f_w_2, w_down_2,
        final_norm_w_2,
    )


_drawn_inputs = setup_inputs


def setup_inputs(seed=0):
    import zlib

    import numpy as np

    out = dict(_drawn_inputs(seed))
    spreads = {}
    factors = {'norm1_g': 5.637,
     'a_sink': 8.0,
     'b_rpb': 8.0,
     'lam_q1': 8.0,
     'lam_k1': 3.196,
     'lam_q2': 3.333,
     'subln_g': 6.189,
     'norm1_w_2': 3.652,
     'conv_a_b_2': 8.0,
     'ln_a_w_2': 21.166,
     'ln_a_b_2': 52.612,
     'lb_gamma_2': 5.688,
     'rec_norm_w_2': 6.145,
     'norm2_w_2': 6.507}
    for name, (base, spread) in spreads.items():
        noise = np.random.default_rng([zlib.crc32(name.encode()), seed]).standard_normal(out[name].shape)
        drawn = base * np.exp(spread * noise) if base else spread * noise
        out[name] = jnp.asarray(drawn.astype(out[name].dtype))
    for name, factor in factors.items():
        out[name] = (out[name] * factor).astype(out[name].dtype)
    return out
```

```python
import math
from contextlib import ExitStack

import numpy as np

import concourse.bass as bass
from concourse import mybir

F32 = mybir.dt.float32
I32 = mybir.dt.int32
ALU = mybir.AluOpType
ACT = mybir.ActivationFunctionType
AX_X = mybir.AxisListType.X

P = 128
D = 1024
KT = D // P
S = 512
C = 256
T = S + C
DH = 64
GRID = 64
ROWS = S // GRID
DFF = 4 * D
HALF = DFF // 2 // P
DFF2 = 2816
NB2 = DFF2 // P
EPS = 1e-6
NEG = -1e30
LAM_INIT = 0.8 - 0.6 * math.exp(-0.3)
TINY = 1e-30
SPLIT = 2.0 ** 60
CONV = 31
PAD = CONV // 2
RING = 8
ARENA_F = 30200
NSLOT = 4
ROT = list(range(16, 32)) + list(range(16))
LEVELS = [1, 2, 4, 8, 16, 32, 64]

SH1, SC1, G1, SH2, SC2, G2 = (i * KT for i in range(6))



class Group:

    def __init__(self, form, weight, chunks, by, role, index, source="h", cols=None, extra=None):
        self.form, self.weight, self.by, self.role, self.index = form, weight, by, role, index
        self.chunks = chunks
        self.source, self.cols, self.extra = source, cols, extra
        self.n = self.first = None

    @property
    def slot(self):
        return self.n % NSLOT

    @property
    def freed_before(self):
        return self.n // NSLOT

    @property
    def done(self):
        return self.first + len(self.chunks)


def full(nb):
    return [(nb, 0, KT)]


def plan():
    phases = []

    def add(kind, layer, groups=(), **more):
        phases.append(dict(kind=kind, layer=layer, groups=list(groups), **more))

    for layer in range(4):
        n_ctx = 2 if layer < 2 else 1
        add("ada", layer, [Group("ada", f"ada{layer}", full(nb), None, "ada", nb, extra=n_ctx) for nb in range(48)])
    for layer in range(2):
        add("norm", layer, which=1, cols=T)
        if layer == 0:
            g = [Group("feat", "even_in", full(nb), "act", "rope_q", nb, cols=T) for nb in range(4)]
            g += [Group("feat", "even_in", full(4), "act", "rope_k", 0, cols=T)]
            g += [Group("tok", "even_in", full(5), "act", "va", 0)]
            g += [Group("feat", "even_in", full(6 + nb), "dve", "plain_q", 4 + nb, cols=T) for nb in range(4)]
            g += [Group("feat", "even_in", full(10), "dve", "plain_k", 1, cols=T)]
            g += [Group("feat", "even_in", full(11), "act", "vbt", 0, cols=T)]
            g += [Group("turn", "even_in", [], "act", "vb", j) for j in range(2)]
        else:
            g = [Group("feat", "odd_in", full(nb), "act", "rope_q", nb, cols=S) for nb in range(8)]
            g += [Group("feat", "odd_in", full(8 + nb), "act", "rope_k", nb, cols=T) for nb in range(8)]
            g += [Group("tok", "odd_in", full(16 + nb), "dve", "v1", nb) for nb in range(8)]
        add("linear", layer, g)
        add("attention", layer)
        cols = T if layer == 0 else S
        add("linear", layer, [Group("feat", f"out{layer}", full(nb), "dve", "residual", nb, source="y", cols=cols, extra=G1)
                              for nb in range(KT)])
        add("norm", layer, which=2, cols=cols)
        for half in range(2):
            add("linear", layer, [Group("feat", f"mlp1_{layer}", full(half * HALF + j), "act", "relu", j, cols=cols)
                                  for j in range(HALF)])
            add("linear", layer, [Group("feat", f"mlp2_{layer}", [(nb, half * HALF, KT), (nb, half * HALF + KT, KT)],
                                        "dve", "residual", nb, source="hid", cols=cols, extra=G2) for nb in range(KT)])
    add("final", 0)
    for layer in (2, 3):
        add("norm", layer, which=1, cols=S)
        w = f"in{layer}"
        g = []
        for j in range(2):
            g += [Group("feat", w, full(2 + j), "act", "gate_a", j, cols=S), Group("feat", w, full(j), "dve", "val_a", j, cols=S)]
        g += [Group("feat", w, full(4 + j), "act", "q2", j, cols=S) for j in range(3)]
        g += [Group("feat", w, full(7 + j), "dve", "k2", j, cols=S) for j in range(3)]
        g += [Group("tok", w, full(10 + j), "act", "v2", j, cols=S) for j in range(3)]
        g += [Group("feat", w, full(13 + j), "act", "silu_q", j, cols=S) for j in range(3)]
        g += [Group("feat", w, full(25 + j), "act", "silu_g", j, cols=S) for j in range(3)]
        g += [Group("feat", w, full(16 + j), "act", "z", j, cols=S) for j in range(6)]
        g += [Group("tok", w, full(22 + j), "dve", "vr", j, cols=S) for j in range(3)]
        add("linear", layer, g)
        add("conv", layer)
        add("attention", layer)
        add("scan", layer)
        add("linear", layer, [Group("feat", f"out{layer}", full(nb), "dve", "residual", nb, source="y", cols=S, extra=G1)
                              for nb in range(KT)])
        add("norm", layer, which=2, cols=S)
        g = []
        for j in range(NB2):
            g += [Group("feat", f"up{layer}", full(j), "act+dve", "ffn_gate", j, cols=S),
                  Group("feat", f"up{layer}", full(NB2 + j), "act+dve", "ffn_val", j, cols=S)]
        add("linear", layer, g)
        add("linear", layer, [Group("feat", f"down{layer}", [(nb, 0, 8), (nb, 8, 8), (nb, 16, 6)],
                                    "dve", "residual", nb, source="hid", cols=S, extra=G2) for nb in range(KT)])
    add("final", 1)
    chunks, n = [], 0
    for ph in phases:
        for g in ph["groups"]:
            g.first = len(chunks)
            chunks += [(g.weight, *c) for c in g.chunks]
            if g.form != "ada":
                g.n = n
                n += 1
    return phases, chunks


def attention_items(layer):
    if layer == 0:
        return ([("a", h, n) for n in range(4) for h in range(8)] + [("b", h, m) for m in range(4) for h in range(8)]
                + [("ca", h, n) for n in range(2) for h in range(8)] + [("cb", h, n) for n in range(2) for h in range(8)])
    if layer == 1:
        return [("d", h, n, m) for n in range(4) for h in range(8) for m in range(2)]
    return [("e", h, n) for n in range(4) for h in range(6)]



def constants():
    t = np.arange(S)
    row, col = (t // GRID).astype(np.float32), (t % GRID).astype(np.float32)
    quarter = DH // 4
    inv = (np.float32(10000.0) ** (-np.arange(quarter, dtype=np.float32) / quarter)).astype(np.float32)
    ar, ac = row[:, None] * inv[None], col[:, None] * inv[None]
    ang = np.concatenate([ar, ar, ac, ac], -1)
    sign = np.where((np.arange(DH) % 32) < 16, -1.0, 1.0)
    cos = np.tile(np.cos(ang).T, (2, 1))
    sin = np.tile((np.sin(ang) * sign).T, (2, 1))
    p, f = np.arange(P)[:, None], np.arange(P)[None]
    win = np.stack([np.where(f >= p, 0.0, NEG), np.where(f <= p, 0.0, NEG)], 1)
    na = np.zeros((P, 3, ROWS, 32), np.float32)
    for v, m in enumerate((0, 1, 3)):
        qc = m * 16 + (np.arange(P) % 16)
        kc = min(max(m * 16 - 8, 0), 32) + np.arange(32)
        cs = np.clip(qc - 8, 0, GRID - 16)
        ok = (kc[None] >= cs[:, None]) & (kc[None] < cs[:, None] + 16)
        na[:, v] = np.where(ok, 0.0, NEG)[:, None, :]
    u = np.arange(896)[None]
    rel = np.abs(p - u + 384)
    count = (rel <= 64).astype(int) + ((rel % 4 == 0) & (rel // 4 <= 64)) + ((rel % 16 == 0) & (rel // 16 <= 64))
    logc = np.where(count > 0, np.log(np.maximum(count, 1)), NEG)
    lev = np.zeros((P, 2, len(LEVELS), 64), np.int32)
    for li, m in enumerate(LEVELS):
        for x in range(64):
            blk = x // m
            s = np.arange(P)
            lev[:, 0, li, x] = (s // (2 * m) == blk) & (s % (2 * m) < m)
            lev[:, 1, li, x] = (s // (2 * m) == blk) & (s % (2 * m) >= m)
    return dict(cos=cos, sin=sin, win=win, na=na.reshape(P, 3, 256), dist=rel * np.ones((P, 1)), logc=logc * np.ones((P, 1)),
                lev=lev, ident=np.eye(P))


SLOPES = [2.0 ** (-8.0 * i / 6) for i in range(1, 7)]


def build(nc, a, out):
    PHASES, CHUNKS = plan()
    with ExitStack() as ctx:
        def sb(name, shape, dt=F32):
            return ctx.enter_context(nc.sbuf_tensor(name, shape, dt))

        def sem(name):
            return ctx.enter_context(nc.semaphore(name))

        ps = ctx.enter_context(nc.psum_tensor("ps", [P, 8, 512], F32))
        psf = ps[:, :, :].rearrange("p b n -> p (b n)")

        ring = sb("ring", [P, RING, KT, P])
        X = sb("resid", [P, KT, T])
        H = sb("hbuf", [P, KT, T])
        ARENA = sb("arena", [P, ARENA_F])
        ones = sb("ones", [P, P])
        ones4 = sb("ones4", [P, P])
        ident = sb("ident", [P, P])
        R = sb("rstd", [P, T])
        mod = sb("mod", [P, 4, 48, 2])
        gs = sb("gs", [P, 4, 2, KT, 2])
        adab = sb("adab", [P, 4, 48])
        gvec = sb("gvec", [P, 4, 2, KT])
        fin_g = sb("fin_g", [P, 2, KT])
        cond = sb("cond", [P, 3, KT])
        sg = sb("sg", [P, 3, KT])
        csil = sb("csil", [P, 3, KT])
        small = sb("small", [P, 64])

        off = [0]

        def carve(n, pattern=None, **k):
            v = ARENA[:, off[0]:off[0] + n]
            off[0] += n
            assert off[0] <= ARENA_F, off[0]
            return v.rearrange(pattern, **k) if pattern else v

        off[0] = 0
        QT = carve(8 * T, "p (b t) -> p b t", b=8)
        KTT = carve(8 * T, "p (b t) -> p b t", b=8)
        VV = carve(6 * 1024, "p (t v) -> p t v", t=6)
        mark = off[0]
        PB = carve(4 * T, "p (s t) -> p s t", s=4)
        PT = carve(2 * T, "p (s t) -> p s t", s=2)
        YT = carve(2 * P, "p (s t) -> p s t", s=2)
        ROTB = PB
        VBT = PB.rearrange("p s t -> p (s t)")[:, 2 * T:2 * T + 1280]
        base_small = off[0]
        off[0] = 8 * T + 2 * T
        BM = carve(8 * 3 * 256, "p (h v k) -> p h v k", h=8, v=3)
        off[0] = base_small
        COS = carve(S)
        SIN = carve(S)
        WIN = carve(2 * P, "p (v k) -> p v k", v=2)
        SINK = carve(8)
        SUBG = carve(1)
        LAMV = carve(4 * DH, "p (v k) -> p v k", v=4)
        LAMS = carve(8)
        SUBT = carve(P)
        after_att = off[0]
        V0 = ARENA[:, 8 * T + 2 * T + 6144:8 * T + 2 * T + 6144 + 16 * P].rearrange("p (t v) -> p t v", t=16)
        assert 8 * T + 2 * T + 6144 + 16 * P <= mark
        off[0] = after_att
        NA = carve(3 * 256, "p (v k) -> p v k", v=3)
        RPBW = carve(8 * 265, "p (h k) -> p h k", h=8)
        off[0] = 0
        HID = carve(NB2 * S, "p (b t) -> p b t", b=NB2)
        HID1 = ARENA[:, 0:HALF * T].rearrange("p (b t) -> p b t", b=HALF)
        off[0] = max(HALF * T, NB2 * S)
        UG = carve(2 * S, "p (s t) -> p s t", s=2)
        UV = carve(2 * S, "p (s t) -> p s t", s=2)
        CFW = carve(3 * 2 * NB2, "p (b k) -> p b k", k=3)
        GL = carve(2 * S, "p (s t) -> p s t", s=2)
        off[0] = 0
        Q2 = carve(3 * S, "p (b t) -> p b t", b=3)
        K2 = carve(3 * S, "p (b t) -> p b t", b=3)
        V2 = carve(4 * 384, "p (t v) -> p t v", t=4)
        QR = carve(3 * S, "p (b t) -> p b t", b=3)
        GR = carve(3 * S, "p (b t) -> p b t", b=3)
        VR = carve(4 * 384, "p (t v) -> p t v", t=4)
        KR = carve(6 * S, "p (b t) -> p b t", b=6)
        LF = carve(6 * S, "p (b t) -> p b t", b=6)
        at_conv = off[0]
        SGA = carve(2 * S, "p (b t) -> p b t", b=2)
        AP_ = carve(2 * (S + 2 * PAD), "p (b t) -> p b t", b=2)
        AC = carve(2 * S, "p (b t) -> p b t", b=2)
        AQ = carve(2 * S, "p (b t) -> p b t", b=2)
        at_att2 = off[0]
        off[0] = at_conv
        BIAS = carve(6 * 896, "p (h k) -> p h k", h=6)
        PB2 = carve(2 * T, "p (s t) -> p s t", s=2)
        PT2 = carve(2 * T, "p (s t) -> p s t", s=2)
        YT2 = carve(2 * P, "p (s t) -> p s t", s=2)
        end1 = off[0]
        off[0] = at_conv
        E = carve(6 * 4 * 129, "p (b t k) -> p b t k", b=6, t=4)
        WL = carve(14 * S, "p (v t) -> p v t", v=14)
        QF = carve(2 * S, "p (v t) -> p v t", v=2)
        KF = carve(2 * S, "p (v t) -> p v t", v=2)
        QX = carve(6 * P, "p (v t) -> p v t", v=6)
        KS = carve(S)
        ET = carve(6)
        end2 = off[0]
        AM = ARENA[:, 0:4 * S].rearrange("p (j t) -> p j t", j=4)
        AMD = ARENA[:, 0:5 * S].rearrange("p (t r) -> p t r", r=S + P)[:, :, 0:P]
        SQR = ARENA[:, 4 * S:4 * S + 256]
        SO = ARENA[:, 4 * S + 512:4 * S + 1024].rearrange("p (t v) -> p t v", t=4)
        off[0] = max(end1, end2, at_att2)
        LEVM = carve(14 * 64, "p (d l k) -> p d l k", d=2, l=7)
        CAW = carve(2 * CONV, "p (b k) -> p b k", b=2)
        CAV = carve(6, "p (b k) -> p b k", b=2)
        GAM = carve(12, "p (d l b) -> p d l b", d=2, l=2)
        LB = carve(6)
        OMLB = carve(6)
        GTMP = carve(24, "p (k b) -> p k b", k=4)
        RNW = carve(3)
        ONE1 = carve(P)

        consts_in = sem("consts_in")
        late_in = sem("late_in")
        w_arrived = [sem(f"w_arrived{i}") for i in range(RING)]
        chunk_done = sem("chunk_done")
        group_freed = [sem(f"group_freed{i}") for i in range(NSLOT)]
        phase_done = sem("phase_done")
        act_chain = sem("act_chain")
        dve_chain = sem("dve_chain")
        pool_chain = sem("pool_chain")
        setup_done = sem("setup_done")
        cond_ready = sem("cond_ready")
        ada_taken = sem("ada_taken")
        sq_ready = sem("sq_ready")
        stats_ready = sem("stats_ready")
        rstd_ready = sem("rstd_ready")
        scaled_ready = sem("scaled_ready")
        rope_in = sem("rope_in")
        rot_ready = sem("rot_ready")
        rot_scaled = sem("rot_scaled")
        rope_out = sem("rope_out")
        relu_ready = sem("relu_ready")
        scores_ready = sem("scores_ready")
        max_ready = sem("max_ready")
        probs_ready = sem("probs_ready")
        probs_mixed = sem("probs_mixed")
        inv_ready = sem("inv_ready")
        pt_ready = sem("pt_ready")
        pt_copied_act = sem("pt_copied_act")
        pt_copied_dve = sem("pt_copied_dve")
        o_ready = sem("o_ready")
        y_ready = sem("y_ready")
        yt_ready = sem("yt_ready")
        yt_taken = sem("yt_taken")
        conv_first = sem("conv_first")
        conv_out = sem("conv_out")
        gelu_ready = sem("gelu_ready")
        hid_ready = sem("hid_ready")
        sig_ready = sem("sig_ready")
        conv_ready = sem("conv_ready")
        ln_step = sem("ln_step")
        ln_mean = sem("ln_mean")
        ln_x = sem("ln_x")
        diff_ready = sem("diff_ready")
        decay_ready = sem("decay_ready")
        levels_ready = sem("levels_ready")
        cross_ready = sem("cross_ready")
        blk_used = sem("blk_used")
        pair_ready = sem("pair_ready")
        pair_taken = sem("pair_taken")
        level_ready = sem("level_ready")
        level_taken = sem("level_taken")
        so_ready = sem("so_ready")
        so_taken = sem("so_taken")
        sosq_ready = sem("sosq_ready")
        sor_ready = sem("sor_ready")
        sy_ready = sem("sy_ready")
        syt_ready = sem("syt_ready")
        syt_taken = sem("syt_taken")
        out_ready = sem("out_ready")
        out_stored = sem("out_stored")
        layer_in = sem("layer_in")
        vbt_ready = sem("vbt_ready")
        vb_turned = sem("vb_turned")
        second_scaled = sem("second_scaled")
        lam_sums = sem("lam_sums")
        lam_exp = sem("lam_exp")
        gam_ready = sem("gam_ready")
        gam_exp = sem("gam_exp")
        o_squares = sem("o_squares")
        o_inv = sem("o_inv")
        so_inv = sem("so_inv")
        gate_clamped = sem("gate_clamped")
        log_ready = sem("log_ready")
        pool_step = sem("pool_step")

        block = ctx.enter_context(nc.Block())

        class Chain:

            def __init__(self, eng, s):
                self.eng, self.sem, self.n = eng, s, 0

            def __call__(self, ins):
                self.n += 1
                ins.then_inc(self.sem, 1)
                self.eng.wait_ge(self.sem, self.n)

        def end_phase(eng, i):
            eng.drain().then_inc(phase_done, 1)
            eng.wait_ge(phase_done, 4 * (i + 1))

        ATT = {layer: attention_items(layer) for layer in range(4)}
        att_base, n_att = {}, 0
        for ph in PHASES:
            if ph["kind"] == "attention":
                att_base[ph["layer"]] = n_att
                n_att += len(ATT[ph["layer"]])

        def value_items(layer):
            its = ATT[layer]
            return its if layer != 1 else its[::2]

        val_base, n_val = {}, 0
        pt2_base, n_pt2 = {}, 0
        yt_base, n_yt = {}, 0

        def key_tiles(item):
            kind = item[0]
            if kind == "a":
                return 5 if 0 < item[2] < 3 else 4
            return {"b": 4, "ca": 2, "cb": 2, "d": 6, "e": 4}[kind]

        for ph in PHASES:
            if ph["kind"] == "attention":
                layer = ph["layer"]
                val_base[layer], pt2_base[layer], yt_base[layer] = n_val, n_pt2, n_yt
                n_val += len(value_items(layer))
                n_pt2 += sum(key_tiles(i) > 4 for i in value_items(layer))
                n_yt += len(value_items(layer)) // (2 if layer != 1 else 1)
        mixed_base = 0

        @block.sync
        def _(sp):
            def load(dst, src, s=consts_in):
                sp.dma_start(dst, src).then_inc(s, 16)

            load(cond[:], a["cond"])
            load(adab[:], a["ada_b"])
            load(gvec[:], a["norm_g"])
            load(fin_g[:], a["fin_g"])
            load(ident[:], a["ident"])
            for kt in range(KT):
                load(X[:, kt, :], a["xT"][kt])

            def chunk(c):
                name, nb, k0, nk = CHUNKS[c]
                if c >= RING:
                    sp.wait_ge(chunk_done, c - RING + 1)
                sp.dma_start(ring[:, c % RING, 0:nk, :], a[name][nb, :, k0:k0 + nk, :]).then_inc(w_arrived[c % RING], 16)

            c = 0
            for i, ph in enumerate(PHASES):
                for g in ph["groups"]:
                    for _ in g.chunks:
                        chunk(c)
                        c += 1
            for kt in range(KT):
                sp.wait_ge(out_ready, kt + 1)
                sp.dma_start(out[kt], H[:, kt, 0:S]).then_inc(out_stored, 16)
            sp.wait_ge(out_stored, 16 * KT)

        def sources(g):
            return {"h": H, "y": H, "hid": HID1 if g.weight.startswith("mlp") else HID}[g.source]

        def product(pe, g):
            slot = psf[:, g.slot * 1024:(g.slot + 1) * 1024]
            if g.n >= NSLOT:
                pe.wait_ge(group_freed[g.slot], g.freed_before)
            src = sources(g)
            if g.form == "turn":
                pe.wait_ge(vbt_ready, 1)
                for t in range(8 * g.index, min(8 * g.index + 8, 10)):
                    mm = nc.tensor.transpose(slot[:, (t % 8) * P:(t % 8 + 1) * P], VBT[:, t * P:(t + 1) * P], ident[:, :])
                mm.then_inc(vb_turned, 1)
                return
            nkt = sum(n for _, _, n in g.chunks)
            if g.form == "feat":
                kt = 0
                for ci, (_, _, n) in enumerate(g.chunks):
                    c = g.first + ci
                    pe.wait_ge(w_arrived[c % RING], 16 * (c // RING + 1))
                    for k in range(n):
                        for lo, hi in ((0, S), (S, T)):
                            if lo >= g.cols:
                                continue
                            mm = nc.tensor.matmul(slot[:, lo:hi], ring[:, c % RING, k, :], src[:, kt, lo:hi],
                                                  start=kt == 0, stop=kt == nkt - 1)
                        kt += 1
                    mm.then_inc(chunk_done, 1)
                return
            c = g.first
            pe.wait_ge(w_arrived[c % RING], 16 * (c // RING + 1))
            if g.form == "tok":
                tiles = [src[:, :, t * P:(t + 1) * P] for t in range((g.cols or T) // P)]
            for t, lhs in enumerate(tiles):
                for k in range(KT):
                    mm = nc.tensor.matmul(slot[:, t * P:(t + 1) * P], lhs[:, k], ring[:, c % RING, k, :],
                                          start=k == 0, stop=k == KT - 1)
            mm.then_inc(chunk_done, 1)

        def phase_index(kind, layer, nth=0):
            return [i for i, ph in enumerate(PHASES) if ph["kind"] == kind and ph["layer"] == layer][nth]

        first0 = phase_index("norm", 0)
        first1 = phase_index("norm", 1)
        first23 = [phase_index("norm", 2), phase_index("norm", 3)]
        up23 = [phase_index("norm", 2, 1), phase_index("norm", 3, 1)]
        att23 = [phase_index("attention", 2), phase_index("attention", 3)]
        first_loads = [first0, first1] + first23 + up23 + att23
        n_loads = {first0: 5 + ROWS, first1: 4, **{i: 5 for i in first23}, **{i: 1 for i in up23}, **{i: 2 for i in att23}}

        def loads_until(i):
            return 16 * sum(n for j, n in n_loads.items() if j <= i)

        N_CONST = 16 * (5 + KT)

        rope_groups = [g for ph in PHASES for g in ph["groups"] if g.role.startswith("rope")]
        relu_groups = [g for ph in PHASES for g in ph["groups"] if g.role == "relu"]
        ffn_groups = [g for ph in PHASES for g in ph["groups"] if g.role.startswith("ffn")]
        gate_groups = [g for ph in PHASES for g in ph["groups"] if g.role == "gate_a"]
        norm_phases = [i for i, ph in enumerate(PHASES) if ph["kind"] in ("norm", "final")]
        conv_phases = [i for i, ph in enumerate(PHASES) if ph["kind"] == "conv"]
        rstd_order = sorted(norm_phases + conv_phases)
        scaled_before = {i: KT * sum(j < i and PHASES[j]["kind"] == "norm" for j in norm_phases) for i in norm_phases}
        scan_phases = [i for i, ph in enumerate(PHASES) if ph["kind"] == "scan"]

        def ranges(cols):
            return [(0, S, 0), (S, T, 1)][:1 if cols == S else 2]

        def pieces(layer, item):
            kind, h, n = item[:3]
            if layer == 0:
                if kind in ("a", "ca"):
                    p0, blk, kb, kv = 64 * (h // 4), h % 4, 0, h // 4
                else:
                    p0, blk, kb, kv = 64 * (h // 4), 4 + h % 4, 1, h // 4
                q, k = QT[p0:p0 + 64, blk], KTT[p0:p0 + 64, kb]
                vs = slice(64 * kv, 64 * kv + 64)
                if kind == "a":
                    lo, hi = max(n - 1, 0), min(n + 1, 3)
                    two = min(lo + 2, hi + 1)
                    ks = [(k[:, S:T], 0), (k[:, lo * P:two * P], C)]
                    if hi + 1 > two:
                        ks.append((k[:, hi * P:(hi + 1) * P], 512))
                    v = [V0[:, 4, vs], V0[:, 5, vs]] + [V0[:, t, vs] for t in range(lo, hi + 1)]
                    return q[:, n * P:(n + 1) * P], ks, v
                if kind == "b":
                    c0 = (0, 8, 24, 32)[n]
                    kg = k[:, 0:S].rearrange("p (r c) -> p r c", c=GRID)[:, :, c0:c0 + 32]
                    v = [V0[:, 6 + 2 * n, vs], V0[:, 7 + 2 * n, vs], V0[:, 14, vs], V0[:, 15, vs]]
                    return q[:, n * P:(n + 1) * P], [(kg, 0), (k[:, S:T], C)], v
                vt = (4, 5) if kind == "ca" else (14, 15)
                return q[:, S + n * P:S + (n + 1) * P], [(k[:, S:T], 0)], [V0[:, t, vs] for t in vt]
            if layer == 1:
                m = item[3]
                q, k = QT[64 * m:64 * m + 64, h], KTT[64 * m:64 * m + 64, h]
                return q[:, n * P:(n + 1) * P], [(k[:, 0:512], 0), (k[:, 512:T], 512)], [V1[:, t, h * P:(h + 1) * P] for t in range(6)]
            p0, blk = 64 * (h % 2), h // 2
            return (Q2[p0:p0 + 64, blk, n * P:(n + 1) * P], [(K2[p0:p0 + 64, blk, :], 0)],
                    [V2[:, t, 64 * h:64 * h + 64] for t in range(4)])

        V1 = VV

        def y_target(layer, pair):
            its = value_items(layer)
            kind, h, n = (its[pair] if layer == 1 else its[2 * pair])[:3]
            if layer == 0:
                blk = h // 2 + (4 if kind in ("b", "cb") else 0)
                if kind == "a":
                    return H[:, blk, n * P:(n + 1) * P]
                if kind == "b":
                    return H[:, blk, 0:S].rearrange("p (r c) -> p r c", c=GRID)[:, :, 16 * n:16 * n + 16]
                return H[:, blk, S + n * P:S + (n + 1) * P]
            if layer == 1:
                return H[:, h, n * P:(n + 1) * P]
            return H[:, 2 + h // 2, n * P:(n + 1) * P]

        def buffers(layer):
            return (PB, PT, YT) if layer < 2 else (PB2, PT2, YT2)

        def s_slot(i):
            return psf[:, (i % 2) * 1024:(i % 2) * 1024 + 1024]

        PT_BANK = (4, 5)
        O_BANK, Y_BANK = 6, 7

        @block.tensor
        def _(pe):
            def attention(layer):
                its, vals = ATT[layer], value_items(layer)
                base, vbase, p2, ybase = att_base[layer], val_base[layer], pt2_base[layer], yt_base[layer]
                pb, pt, yt = buffers(layer)
                per = 2 if layer == 1 else 1
                dv = P if layer == 1 else 64
                seconds = [sum(key_tiles(v) > 4 for v in vals[:j + 1]) for j in range(len(vals))]

                def scores(i):
                    q, ks, _ = pieces(layer, its[i])
                    if i >= 2:
                        pe.wait_ge(probs_ready, base + i - 1)
                    for k, off_ in ks:
                        n = 1
                        for d in k.shape[1:]:
                            n *= d
                        mm = nc.tensor.matmul(s_slot(i)[:, off_:off_ + n], q, k, start=True, stop=True)
                    mm.then_inc(scores_ready, 1)

                def turn(j):
                    nt = key_tiles(vals[j])
                    if layer == 1:
                        pe.wait_ge(probs_mixed, j + 1)
                    else:
                        pe.wait_ge(probs_ready, base + j + 1)
                    if j >= 1:
                        pe.wait_ge(pt_copied_act, vbase + j)
                        if seconds[j - 1]:
                            pe.wait_ge(pt_copied_dve, p2 + seconds[j - 1])
                    for t in range(nt):
                        src = pb[:, 2 * (j % 2) if layer == 1 else j % 2, t * P:(t + 1) * P]
                        mm = nc.tensor.transpose(ps[:, PT_BANK[t // 4], (t % 4) * P:(t % 4 + 1) * P], src, ident[:, :])
                    mm.then_inc(pt_ready, 1)

                def values(j):
                    nt = key_tiles(vals[j])
                    vt = pieces(layer, vals[j] if layer != 1 else vals[j])[2]
                    pe.wait_ge(pt_copied_act, vbase + j + 1)
                    if nt > 4:
                        pe.wait_ge(pt_copied_dve, p2 + seconds[j])
                    if j >= 1:
                        pe.wait_ge(y_ready, vbase + j)
                    for t in range(nt):
                        mm = nc.tensor.matmul(ps[:, O_BANK, (j % 2) * P:(j % 2) * P + dv], pt[:, j % 2, t * P:(t + 1) * P],
                                              vt[t], start=t == 0, stop=t == nt - 1)
                    mm.then_inc(o_ready, 1)

                def turn_y(y):
                    pe.wait_ge(y_ready, vbase + (y + 1) * (1 if layer == 1 else 2))
                    if y >= 1:
                        pe.wait_ge(yt_taken, ybase + y)
                    nc.tensor.transpose(ps[:, Y_BANK, (y % 2) * P:(y % 2 + 1) * P], yt[:, y % 2, :], ident[:, :]).then_inc(yt_ready, 1)

                nv = len(vals)
                ys = {(2 * y + 1 if per == 1 else y): y for y in range(nv if per == 2 else nv // 2)}
                for j in range(nv + 3):
                    if j < nv:
                        for i in range(per * j, per * j + per):
                            scores(i)
                    if 1 <= j <= nv:
                        turn(j - 1)
                    if 2 <= j <= nv + 1:
                        values(j - 2)
                    if j >= 3 and j - 3 in ys:
                        turn_y(ys[j - 3])

            def norm(i, cols):
                n = norm_phases.index(i)
                for kt in range(KT):
                    pe.wait_ge(sq_ready, KT * n + kt + 1)
                    for lo, hi, _ in ranges(cols):
                        mm = nc.tensor.matmul(psf[:, lo:hi], ones[:], H[:, kt, lo:hi], start=kt == 0, stop=kt == KT - 1)
                mm.then_inc(stats_ready, 1)

            def conv(i):
                n = conv_phases.index(i)
                pe.wait_ge(conv_ready, 2 * n + 2)
                for b in range(2):
                    mm = nc.tensor.matmul(ps[:, 0, :], ones4[:], AC[:, b, :], start=b == 0, stop=b == 1)
                mm.then_inc(ln_mean, 1)
                pe.wait_ge(ln_step, n + 1)
                for b in range(2):
                    mm = nc.tensor.matmul(ps[:, 1, :], ones4[:], AQ[:, b, :], start=b == 0, stop=b == 1)
                mm.then_inc(ln_mean, 1)

            def scan(i):
                n = scan_phases.index(i)
                for h in range(6):
                    hh, b, p0 = 6 * n + h, h // 2, 64 * (h % 2)
                    rows = slice(p0, p0 + 64)
                    if h % 2 == 0:
                        pe.wait_ge(cross_ready, 3 * n + b + 1)
                    for j in range(4):
                        if 4 * hh + j >= 2:
                            pe.wait_ge(pair_taken, 4 * hh + j - 1)
                        for t in range(4):
                            o = ps[:, j % 2, t * P:(t + 1) * P]
                            if t == j:
                                lhs, rhs = KS[rows, j * P:(j + 1) * P], QR[rows, b, t * P:(t + 1) * P]
                            elif t > j:
                                x = {(2, 0): 0, (3, 1): 1, (3, 0): 2}.get((t, j))
                                lhs = KF[rows, 0, j * P:(j + 1) * P]
                                rhs = QF[rows, 0, t * P:(t + 1) * P] if x is None else QX[rows, x, :]
                            else:
                                x = {(1, 3): 4, (0, 2): 3, (0, 3): 5}.get((t, j))
                                lhs = KF[rows, 1, j * P:(j + 1) * P]
                                rhs = QF[rows, 1, t * P:(t + 1) * P] if x is None else QX[rows, x, :]
                            mm = nc.tensor.matmul(o, lhs, rhs, start=True, stop=True)
                        mm.then_inc(pair_ready, 1)
                    if h % 2 == 0:
                        pe.wait_ge(levels_ready, 3 * n + b + 1)
                    for dl in range(14):
                        d, m = dl // 7, LEVELS[dl % 7]
                        if 14 * hh + dl >= 2:
                            pe.wait_ge(level_taken, 14 * hh + dl - 1)
                        for t in range(4):
                            w = WL[rows, dl, t * P:(t + 1) * P]
                            q = w.rearrange("p (b x m) -> p x b m", x=2, m=m)[:, 1 - d]
                            mm = nc.tensor.matmul(ps[:, 2 + dl % 2, t * 64:(t + 1) * 64], w, q, start=True, stop=True)
                        mm.then_inc(level_ready, 1)
                    pe.wait_ge(level_taken, 14 * hh + 14)
                    pe.wait_ge(pair_taken, 4 * hh + 4)
                    if hh >= 1:
                        pe.wait_ge(so_taken, hh)
                    for t in range(4):
                        for j in range(4):
                            mm = nc.tensor.matmul(ps[:, 4, t * 64:(t + 1) * 64], AM[:, j, t * P:(t + 1) * P],
                                                  VR[:, j, 64 * h:64 * h + 64], start=j == 0, stop=j == 3)
                    mm.then_inc(so_ready, 1)
                    if h % 2 == 1:
                        pe.wait_ge(sy_ready, hh + 1)
                        if 3 * n + b >= 1:
                            pe.wait_ge(syt_taken, 3 * n + b)
                        for t in range(4):
                            mm = nc.tensor.transpose(ps[:, 5, t * P:(t + 1) * P], SO[:, t, :], ident[:, :])
                        mm.then_inc(syt_ready, 1)

            def ada(ph):
                layer = ph["layer"]
                if layer == 0:
                    pe.wait_ge(cond_ready, 1)
                if layer >= 1:
                    pe.wait_ge(ada_taken, layer)
                for g in ph["groups"]:
                    c = g.first
                    pe.wait_ge(w_arrived[c % RING], 16 * (c // RING + 1))
                    w = g.extra
                    for k in range(KT):
                        v = csil[:, 0:2, k] if layer < 2 else csil[:, 2:3, k]
                        mm = nc.tensor.matmul(ps[:, 0, w * g.index:w * g.index + w], ring[:, c % RING, k, :], v,
                                              start=k == 0, stop=k == KT - 1)
                    mm.then_inc(chunk_done, 1)

            pe.wait_ge(consts_in, N_CONST)
            pe.wait_ge(setup_done, 1)
            for i, ph in enumerate(PHASES):
                kind, layer = ph["kind"], ph["layer"]
                if kind == "ada":
                    ada(ph)
                elif kind == "norm":
                    norm(i, ph["cols"])
                elif kind == "final":
                    norm(i, S)
                elif kind == "linear":
                    for g in ph["groups"]:
                        product(pe, g)
                elif kind == "attention":
                    attention(layer)
                elif kind == "conv":
                    conv(i)
                elif kind == "scan":
                    scan(i)
                end_phase(pe, i)


        @block.scalar
        def _(act):
            chain = Chain(act, act_chain)

            def take(g):
                slot = psf[:, g.slot * 1024:(g.slot + 1) * 1024]
                if g.form == "turn":
                    act.wait_ge(vb_turned, g.index + 1)
                else:
                    act.wait_ge(chunk_done, g.done)
                freed = group_freed[g.slot]
                role, j = g.role, g.index
                if role == "rope_q":
                    nc.scalar.activation(QT[:, j, 0:g.cols], slot[:, 0:g.cols], ACT.Copy, scale=0.125).then_inc(freed, 1)
                    act.drain().then_inc(rope_in, 1)
                elif role == "rope_k":
                    nc.scalar.activation(KTT[:, j, 0:T], slot[:, 0:T], ACT.Copy).then_inc(freed, 1)
                    act.drain().then_inc(rope_in, 1)
                elif role == "va":
                    nc.scalar.activation(V0[:, 0:6, :], slot[:, 0:768].rearrange("p (t v) -> p t v", t=6), ACT.Copy).then_inc(freed, 1)
                elif role == "vbt":
                    grid = slot[:, 0:S].rearrange("p (r c) -> p r c", c=GRID)
                    for m, c0 in enumerate((0, 8, 24, 32)):
                        nc.scalar.activation(VBT[:, m * 256:(m + 1) * 256].rearrange("p (r c) -> p r c", c=32), grid[:, :, c0:c0 + 32], ACT.Copy)
                    nc.scalar.activation(VBT[:, 1024:1280], slot[:, S:T], ACT.Copy).then_inc(freed, 1)
                    act.drain().then_inc(vbt_ready, 1)
                elif role == "vb":
                    n = 8 if j == 0 else 2
                    nc.scalar.activation(V0[:, 6 + 8 * j:6 + 8 * j + n, :], slot[:, 0:n * P].rearrange("p (t v) -> p t v", t=n), ACT.Copy).then_inc(freed, 1)
                elif role == "relu":
                    nc.scalar.activation(HID1[:, j, 0:g.cols], slot[:, 0:g.cols], ACT.Relu).then_inc(freed, 1)
                    act.drain().then_inc(relu_ready, 1)
                elif role == "gate_a":
                    nc.scalar.activation(SGA[:, j, :], slot[:, 0:S], ACT.Sigmoid).then_inc(freed, 1)
                    act.drain().then_inc(sig_ready, 1)
                elif role == "q2":
                    nc.scalar.activation(Q2[:, j, :], slot[:, 0:S], ACT.Copy, scale=0.125).then_inc(freed, 1)
                elif role == "v2":
                    nc.scalar.activation(V2[:, :, j * P:(j + 1) * P], slot[:, 0:S].rearrange("p (t v) -> p t v", t=4), ACT.Copy).then_inc(freed, 1)
                elif role in ("silu_q", "silu_g"):
                    dst = QR if role == "silu_q" else GR
                    nc.scalar.activation(dst[:, j, :], slot[:, 0:S], ACT.Silu).then_inc(freed, 1)
                elif role == "z":
                    nc.scalar.activation(LF[:, j, :], slot[:, 0:S], ACT.Sigmoid)
                    nc.scalar.activation(KR[:, j, :], slot[:, 0:S], ACT.Sigmoid, scale=-1.0).then_inc(freed, 1)
                elif role.startswith("ffn"):
                    n = ffn_groups.index(g)
                    blk = j if role == "ffn_gate" else NB2 + j
                    u = (UG if role == "ffn_gate" else UV)[:, j % 2, :]
                    if n >= 4:
                        act.wait_ge(hid_ready, n // 2 - 1)
                    nc.scalar.activation(u, slot[:, 0:S], ACT.Copy, scale=CFW[:, blk, 1:2]).then_inc(conv_first, 1)
                    if role == "ffn_val" and j >= 1:
                        gelu(n // 2 - 1)
                    if role == "ffn_val" and j == NB2 - 1:
                        gelu(n // 2)

            def gelu(n):
                act.wait_ge(conv_out, 2 * n + 1)
                if n >= 2:
                    act.wait_ge(hid_ready, n - 1)
                nc.scalar.activation(GL[:, n % 2, :], UG[:, n % 2, :], ACT.Gelu).then_inc(gelu_ready, 1)

            def attention(layer):
                its, vals = ATT[layer], value_items(layer)
                base, vbase, ybase = att_base[layer], val_base[layer], yt_base[layer]
                pb, pt, yt = buffers(layer)
                per = 2 if layer == 1 else 1

                def probs(i):
                    item = its[i]
                    n = key_tiles(item) * P
                    act.wait_ge(max_ready, base + i + 1)
                    if layer != 1 and i >= 2:
                        act.wait_ge(pt_ready, vbase + i - 1)
                    if layer == 1 and i >= 4:
                        act.wait_ge(pt_ready, vbase + i // 2 - 1)
                    if item[0] in ("a", "ca"):
                        nc.scalar.activation(small[:, 8 + i % 4:9 + i % 4], SINK[:, item[1]:item[1] + 1], ACT.Exp,
                                             bias=small[:, i % 4:i % 4 + 1])
                    nc.scalar.activation(pb[:, i % 4 if layer == 1 else i % 2, 0:n], s_slot(i)[:, 0:n], ACT.Exp, bias=small[:, i % 4:i % 4 + 1],
                                         accum_out=small[:, 4 + i % 4:5 + i % 4]).then_inc(probs_ready, 1)

                def copy_pt(j):
                    n = min(key_tiles(vals[j]), 4) * P
                    act.wait_ge(pt_ready, vbase + j + 1)
                    if j >= 2:
                        act.wait_ge(o_ready, vbase + j - 1)
                    nc.scalar.activation(pt[:, j % 2, 0:n], ps[:, PT_BANK[0], 0:n], ACT.Copy).then_inc(pt_copied_act, 1)

                def take_o(j):
                    act.wait_ge(o_ready, vbase + j + 1)
                    pair = j if layer == 1 else j // 2
                    if layer == 1:
                        if pair >= 2:
                            act.wait_ge(yt_ready, ybase + pair - 1)
                        o = ps[:, O_BANK, (j % 2) * P:(j % 2 + 1) * P]
                        nc.scalar.activation(SUBT, o, ACT.Square, scale=P ** -0.5,
                                             accum_out=small[:, 20 + j % 2:21 + j % 2]).then_inc(o_squares, 1)
                        act.wait_ge(o_inv, j + 1)
                        nc.scalar.activation(yt[:, j % 2, :], o, ACT.Copy, scale=small[:, 24 + j % 2:25 + j % 2]).then_inc(y_ready, 1)
                        return
                    act.wait_ge(inv_ready, base + j + 1)
                    if j % 2 == 0 and pair >= 2:
                        act.wait_ge(yt_ready, ybase + pair - 1)
                    nc.scalar.activation(yt[:, pair % 2, 64 * (j % 2):64 * (j % 2) + 64], ps[:, O_BANK, (j % 2) * P:(j % 2) * P + 64],
                                         ACT.Copy, scale=small[:, 12 + j % 4:13 + j % 4]).then_inc(y_ready, 1)

                nv = len(vals)
                for j in range(nv + 2):
                    if j < nv:
                        for i in range(per * j, per * j + per):
                            probs(i)
                    if 1 <= j <= nv:
                        copy_pt(j - 1)
                    if j >= 2:
                        take_o(j - 2)

            def norm(i, ph, final):
                n = norm_phases.index(i)
                cols = S if final else ph["cols"]
                layer = ph["layer"]
                for kt in range(KT):
                    nc.scalar.activation(H[:, kt, 0:cols], X[:, kt, 0:cols], ACT.Square).then_inc(sq_ready, 1)
                act.wait_ge(stats_ready, n + 1)
                nc.scalar.activation(R[:, 0:cols], psf[:, 0:cols], ACT.Sqrt, bias=small[:, 40:41]).then_inc(rstd_ready, 1)
                if final:
                    return
                for kt in range(KT):
                    for lo, hi, s in ranges(cols):
                        act.wait_ge(scaled_ready, scaled_before[i] + kt + 1)
                        nc.scalar.activation(H[:, kt, lo:hi], H[:, kt, lo:hi], ACT.Identity,
                                             scale=gs[:, layer, ph["which"] - 1, kt, s:s + 1],
                                             bias=mod[:, layer, (SH1 if ph["which"] == 1 else SH2) + kt, s:s + 1])

            def conv(i):
                n = conv_phases.index(i)
                for b in range(2):
                    act.wait_ge(ln_x, 3 * n + 1)
                    nc.scalar.activation(AQ[:, b, :], AC[:, b, :], ACT.Square)
                act.drain().then_inc(ln_step, 1)
                act.wait_ge(ln_mean, 2 * n + 2)
                nc.scalar.activation(R[:, 0:S], ps[:, 1, :], ACT.Sqrt, bias=small[:, 40:41]).then_inc(rstd_ready, 1)
                for b in range(2):
                    act.wait_ge(ln_x, 3 * n + 2 + b)
                    nc.scalar.activation(H[:, b, 0:S], AC[:, b, :], ACT.Silu, scale=CAV[:, b, 1:2], bias=CAV[:, b, 2:3])

            def scan(i):
                n = scan_phases.index(i)
                for b in range(6):
                    act.wait_ge(gate_clamped, 6 * n + b + 1)
                    nc.scalar.activation(LF[:, b, :], LF[:, b, :], ACT.Ln)
                    nc.scalar.activation(WL[:, b, :], WL[:, b, :], ACT.Ln).then_inc(log_ready, 1)
                for b in range(3):
                    act.wait_ge(diff_ready, 3 * n + b + 1)
                    for d in range(2):
                        nc.scalar.activation(WL[:, 7 * d:7 * d + 7, :], WL[:, 7 * d:7 * d + 7, :], ACT.Exp)
                    nc.scalar.activation(QF[:], QF[:], ACT.Exp)
                    nc.scalar.activation(KF[:], KF[:], ACT.Exp)
                    nc.scalar.activation(ET[:], ET[:], ACT.Exp)
                    act.drain().then_inc(decay_ready, 1)
                    for h in (2 * b, 2 * b + 1):
                        hh = 6 * n + h
                        for j in range(4):
                            act.wait_ge(pair_ready, 4 * hh + j + 1)
                            if j == 0 and hh >= 1:
                                act.wait_ge(so_ready, hh)
                            nc.scalar.activation(AM[:, j, :], ps[:, j % 2, :], ACT.Copy).then_inc(pair_taken, 1)
                        act.wait_ge(so_ready, hh + 1)
                        if hh >= 1:
                            act.wait_ge(sor_ready, hh)
                        nc.scalar.activation(SQR, ps[:, 4, 0:256], ACT.Square, scale=0.125).then_inc(sosq_ready, 1)

            act.wait_ge(consts_in, N_CONST)
            nc.scalar.activation(sg[:], cond[:], ACT.Sigmoid).then_inc(sig_ready, 1)
            act.wait_ge(setup_done, 1)
            for i, ph in enumerate(PHASES):
                kind, layer = ph["kind"], ph["layer"]
                if i in first_loads:
                    act.wait_ge(layer_in, loads_until(i))
                if i == first1:
                    act.wait_ge(lam_sums, 1)
                    nc.scalar.activation(LAMS[:, 2:4], LAMS[:, 0:2], ACT.Exp).then_inc(lam_exp, 1)
                if i in first23:
                    act.wait_ge(gam_ready, first23.index(i) + 1)
                    nc.scalar.activation(GTMP[:, 1:3], GTMP[:, 1:3], ACT.Exp).then_inc(gam_exp, 1)
                if kind == "norm":
                    norm(i, ph, False)
                elif kind == "final":
                    norm(i, ph, True)
                elif kind == "linear":
                    for g in ph["groups"]:
                        if g.by in ("act", "act+dve"):
                            take(g)
                elif kind == "attention":
                    attention(layer)
                elif kind == "conv":
                    conv(i)
                elif kind == "scan":
                    scan(i)
                end_phase(act, i)

        @block.vector
        def _(dve):
            chain = Chain(dve, dve_chain)

            def take(g):
                slot = psf[:, g.slot * 1024:(g.slot + 1) * 1024]
                freed = group_freed[g.slot]
                role, j = g.role, g.index
                if role in ("rope_q", "rope_k"):
                    n = rope_groups.index(g)
                    buf = (QT if role == "rope_q" else KTT)[:, j, 0:S]
                    dve.wait_ge(rope_in, n + 1)
                    nc.vector.stream_shuffle(ROTB[:, n % 2, 0:S], buf, ROT).then_inc(rot_ready, 1)
                    dve.wait_ge(rot_ready, n + 1)
                    chain(nc.vector.tensor_tensor(buf, buf, COS, ALU.mult))
                    dve.wait_ge(rot_scaled, n + 1)
                    nc.vector.tensor_tensor(buf, buf, ROTB[:, n % 2, 0:S], ALU.add).then_inc(rope_out, 1)
                    return
                if role.startswith("ffn"):
                    n = ffn_groups.index(g)
                    blk = j if role == "ffn_gate" else NB2 + j
                    u = (UG if role == "ffn_gate" else UV)[:, j % 2, :]
                    dve.wait_ge(conv_first, n + 1)
                    chain(nc.vector.scalar_tensor_tensor(out=u[:, 1:S], in0=slot[:, 0:S - 1], scalar=CFW[:, blk, 0:1],
                                                         in1=u[:, 1:S], op0=ALU.mult, op1=ALU.add))
                    nc.vector.scalar_tensor_tensor(out=u[:, 0:S - 1], in0=slot[:, 1:S], scalar=CFW[:, blk, 2:3],
                                                   in1=u[:, 0:S - 1], op0=ALU.mult, op1=ALU.add).then_inc(freed, 1)
                    dve.drain().then_inc(conv_out, 1)
                    return
                dve.wait_ge(chunk_done, g.done)
                if role == "plain_q":
                    for m in range(4):
                        nc.vector.tensor_scalar(QT[:, j, m * P:(m + 1) * P].rearrange("p (r c) -> p r c", c=16),
                                                slot[:, 0:S].rearrange("p (r c) -> p r c", c=GRID)[:, :, 16 * m:16 * m + 16],
                                                0.125, None, ALU.mult)
                    nc.vector.tensor_scalar(QT[:, j, S:T], slot[:, S:T], 0.125, None, ALU.mult).then_inc(freed, 1)
                elif role == "plain_k":
                    nc.vector.tensor_copy(KTT[:, j, 0:T], slot[:, 0:T]).then_inc(freed, 1)
                elif role == "v1":
                    nc.vector.tensor_copy(V1[:, :, j * P:(j + 1) * P], slot[:, 0:768].rearrange("p (t v) -> p t v", t=6)).then_inc(freed, 1)
                elif role == "k2":
                    nc.vector.tensor_copy(K2[:, j, :], slot[:, 0:S]).then_inc(freed, 1)
                elif role == "vr":
                    nc.vector.tensor_copy(VR[:, :, j * P:(j + 1) * P], slot[:, 0:S].rearrange("p (t v) -> p t v", t=4)).then_inc(freed, 1)
                elif role == "val_a":
                    n = gate_groups.index([x for x in gate_groups if x.weight == g.weight and x.index == j][0])
                    dve.wait_ge(sig_ready, n + 2)
                    nc.vector.tensor_tensor(AP_[:, j, PAD:PAD + S], slot[:, 0:S], SGA[:, j, :], ALU.mult).then_inc(freed, 1)
                elif role == "residual":
                    rs = ranges(g.cols)
                    layer = int(g.weight[-1])
                    for lo, hi, s in rs:
                        x = nc.vector.scalar_tensor_tensor(out=X[:, j, lo:hi], in0=slot[:, lo:hi], scalar=mod[:, layer, g.extra + j, s:s + 1],
                                                           in1=X[:, j, lo:hi], op0=ALU.mult, op1=ALU.add)
                    x.then_inc(freed, 1)

            def attention(layer):
                its, vals = ATT[layer], value_items(layer)
                base, vbase, ybase = att_base[layer], val_base[layer], yt_base[layer]
                pb, pt, yt = buffers(layer)
                per = 2 if layer == 1 else 1

                def maxima(i):
                    item = its[i]
                    n = key_tiles(item) * P
                    dve.wait_ge(scores_ready, base + i + 1)
                    s = s_slot(i)
                    if item[0] == "a":
                        q = item[2]
                        masks = []
                        if q > 0:
                            masks.append((C, 0))
                        if q < 3:
                            masks.append((C + P if q == 0 else 512, 1))
                        for off_, m in masks:
                            chain(nc.vector.tensor_tensor(s[:, off_:off_ + P], s[:, off_:off_ + P], WIN[:, m, :], ALU.add))
                    if item[0] == "b":
                        v = (0, 1, 1, 2)[item[2]]
                        chain(nc.vector.tensor_tensor(s[:, 0:256], s[:, 0:256], BM[:, item[1], v, :], ALU.add))
                    if item[0] == "e":
                        o = 384 - P * item[2]
                        chain(nc.vector.tensor_tensor(s[:, 0:512], s[:, 0:512], BIAS[:, item[1], o:o + 512], ALU.add))
                    nm = small[:, i % 4:i % 4 + 1]
                    if item[0] in ("a", "ca"):
                        chain(nc.vector.tensor_reduce(small[:, 48 + i % 8:49 + i % 8], s[:, 0:n], AX_X, ALU.max))
                        nc.vector.tensor_scalar(nm, small[:, 48 + i % 8:49 + i % 8], SINK[:, item[1]:item[1] + 1], -1.0, ALU.max, ALU.mult).then_inc(max_ready, 1)
                    else:
                        nc.vector.tensor_reduce(nm, s[:, 0:n], AX_X, ALU.max, negate=True).then_inc(max_ready, 1)

                def inverse(i):
                    item = its[i]
                    dve.wait_ge(probs_ready, base + i + 1)
                    l = small[:, 4 + i % 4:5 + i % 4]
                    inv = small[:, 12 + i % 4:13 + i % 4]
                    if item[0] in ("a", "ca"):
                        chain(nc.vector.tensor_tensor(l, l, small[:, 8 + i % 4:9 + i % 4], ALU.add))
                    if layer == 1 and i % 2:
                        chain(nc.vector.reciprocal(inv, l))
                        nc.vector.tensor_scalar(inv, inv, LAMS[:, 7:8], None, ALU.mult).then_inc(inv_ready, 1)
                    else:
                        nc.vector.reciprocal(inv, l).then_inc(inv_ready, 1)

                def mix(j):
                    n = 6 * P
                    dve.wait_ge(second_scaled, j + 1)
                    dve.wait_ge(inv_ready, base + 2 * j + 2)
                    i0 = 2 * j
                    nc.vector.scalar_tensor_tensor(out=pb[:, 2 * (j % 2), 0:n], in0=pb[:, 2 * (j % 2), 0:n], scalar=small[:, 12 + i0 % 4:13 + i0 % 4],
                                                   in1=pb[:, 2 * (j % 2) + 1, 0:n], op0=ALU.mult, op1=ALU.add).then_inc(probs_mixed, 1)

                def copy_pt(j):
                    n = key_tiles(vals[j])
                    if n <= 4:
                        return
                    dve.wait_ge(pt_ready, vbase + j + 1)
                    if j >= 2:
                        dve.wait_ge(o_ready, vbase + j - 1)
                    nc.vector.tensor_copy(pt[:, j % 2, 512:n * P], ps[:, PT_BANK[1], 0:(n - 4) * P]).then_inc(pt_copied_dve, 1)

                def take_y(y):
                    dve.wait_ge(yt_ready, ybase + y + 1)
                    src = ps[:, Y_BANK, (y % 2) * P:(y % 2 + 1) * P]
                    dst = y_target(layer, y)
                    if layer == 1:
                        nc.vector.tensor_scalar(dst, src, SUBG, 1.0 - LAM_INIT, ALU.mult, ALU.mult).then_inc(yt_taken, 1)
                    else:
                        if len(dst.shape) == 3:
                            src = src.rearrange("p (r c) -> p r c", c=16)
                        nc.vector.tensor_copy(dst, src).then_inc(yt_taken, 1)

                nv = len(vals)
                ys = {(2 * y + 1 if per == 1 else y): y for y in range(nv if per == 2 else nv // 2)}
                for j in range(nv + 3):
                    if j < nv:
                        for i in range(per * j, per * j + per):
                            maxima(i)
                    if layer == 1 and 1 <= j <= nv:
                        inverse(2 * j - 2)
                        inverse(2 * j - 1)
                        mix(j - 1)
                    elif 1 <= j <= nv:
                        inverse(j - 1)
                    if 1 <= j <= nv:
                        copy_pt(j - 1)
                    if j >= 3 and j - 3 in ys:
                        take_y(ys[j - 3])

            def norm(i, ph, final):
                n = rstd_order.index(i)
                cols = S if final else ph["cols"]
                dve.wait_ge(rstd_ready, n + 1)
                chain(nc.vector.reciprocal(R[:, 0:cols], R[:, 0:cols]))
                for kt in range(KT):
                    if not final:
                        nc.vector.tensor_tensor(H[:, kt, 0:cols], X[:, kt, 0:cols], R[:, 0:cols], ALU.mult).then_inc(scaled_ready, 1)
                    elif ph["layer"] == 0:
                        nc.vector.scalar_tensor_tensor(out=X[:, kt, 0:S], in0=X[:, kt, 0:S], scalar=fin_g[:, 0, kt:kt + 1],
                                                       in1=R[:, 0:S], op0=ALU.mult, op1=ALU.mult)
                    else:
                        nc.vector.scalar_tensor_tensor(out=H[:, kt, 0:S], in0=X[:, kt, 0:S], scalar=fin_g[:, 1, kt:kt + 1],
                                                       in1=R[:, 0:S], op0=ALU.mult, op1=ALU.mult).then_inc(out_ready, 1)

            def bias0():
                for v, shift in enumerate((0, -8, -16)):
                    for h in range(8):
                        src = RPBW[:, h, 248 - shift:249 - shift]
                        src = bass.AP(src.tensor, src.offset, [src.ap[0], [-31, 8], [-1, 32]])
                        nc.vector.tensor_tensor(BM[:, h, v, :].rearrange("p (r c) -> p r c", r=8), src,
                                                NA[:, v, :].rearrange("p (r c) -> p r c", r=8), ALU.add)

            def lam1():
                for m in range(2):
                    chain(nc.vector.tensor_tensor(LAMV[:, 2 * m, :], LAMV[:, 2 * m, :], LAMV[:, 2 * m + 1, :], ALU.mult))
                    chain(nc.vector.reduce_sum(LAMS[:, m:m + 1], LAMV[:, 2 * m, :], AX_X))
                dve.drain().then_inc(lam_sums, 1)
                dve.wait_ge(lam_exp, 1)
                chain(nc.vector.tensor_tensor(LAMS[:, 4:5], LAMS[:, 3:4], LAMS[:, 2:3], ALU.subtract))
                chain(nc.vector.tensor_scalar(LAMS[:, 7:8], LAMS[:, 4:5], -LAM_INIT, None, ALU.add))

            def bounds(k):
                g0, g1 = GAM[:, 0].rearrange("p l b -> p (l b)"), GAM[:, 1].rearrange("p l b -> p (l b)")
                chain(nc.vector.tensor_tensor(GTMP[:, 0], g0, g1, ALU.max))
                chain(nc.vector.tensor_tensor(GTMP[:, 1], g0, GTMP[:, 0], ALU.subtract))
                chain(nc.vector.tensor_tensor(GTMP[:, 2], g1, GTMP[:, 0], ALU.subtract))
                dve.drain().then_inc(gam_ready, 1)
                dve.wait_ge(gam_exp, k + 1)
                chain(nc.vector.tensor_tensor(GTMP[:, 0], GTMP[:, 1], GTMP[:, 2], ALU.add))
                chain(nc.vector.reciprocal(GTMP[:, 0], GTMP[:, 0]))
                chain(nc.vector.tensor_tensor(GTMP[:, 1], GTMP[:, 1], GTMP[:, 0], ALU.mult))
                chain(nc.vector.tensor_tensor(GTMP[:, 2], GTMP[:, 2], GTMP[:, 0], ALU.mult))
                if k == 0:
                    chain(nc.vector.tensor_tensor(LB, GTMP[:, 1], GTMP[:, 1], ALU.subtract))
                else:
                    chain(nc.vector.tensor_tensor(GTMP[:, 2], GTMP[:, 1], GTMP[:, 2], ALU.add))
                    chain(nc.vector.tensor_tensor(LB, GTMP[:, 2], GTMP[:, 1], ALU.subtract))
                chain(nc.vector.tensor_scalar(OMLB, LB, -1.0, 1.0, ALU.mult, ALU.add))

            def conv(i):
                n = conv_phases.index(i)
                for b in range(2):
                    chain(nc.vector.tensor_scalar(AC[:, b, :], AP_[:, b, 0:S], CAW[:, b, 0:1], CAV[:, b, 0:1], ALU.mult, ALU.add))
                for t in range(1, CONV):
                    for b in range(2):
                        x = nc.vector.scalar_tensor_tensor(out=AC[:, b, :], in0=AP_[:, b, t:t + S], scalar=CAW[:, b, t:t + 1],
                                                           in1=AC[:, b, :], op0=ALU.mult, op1=ALU.add)
                        if t == CONV - 1:
                            x.then_inc(conv_ready, 1)
                        elif b == 1:
                            chain(x)
                dve.wait_ge(ln_mean, 2 * n + 1)
                dve.wait_ge(conv_ready, 2 * n + 2)
                for b in range(2):
                    x = nc.vector.tensor_tensor(AC[:, b, :], AC[:, b, :], ps[:, 0, :], ALU.subtract)
                x.then_inc(ln_x, 1)
                dve.wait_ge(ln_x, 3 * n + 1)
                dve.wait_ge(rstd_ready, rstd_order.index(i) + 1)
                chain(nc.vector.reciprocal(R[:, 0:S], R[:, 0:S]))
                for b in range(2):
                    nc.vector.tensor_tensor(AC[:, b, :], AC[:, b, :], R[:, 0:S], ALU.mult).then_inc(ln_x, 1)

            def bias2():
                for h in (5, 4, 3, 2):
                    nc.vector.scalar_tensor_tensor(out=BIAS[:, h, :], in0=BIAS[:, 0, :], scalar=-SLOPES[h], in1=BIAS[:, 1, :],
                                                   op0=ALU.mult, op1=ALU.add)
                chain(nc.vector.tensor_copy(PB2[:, 0:2, :].rearrange("p s t -> p (s t)")[:, 0:896], BIAS[:, 0, :]))
                chain(nc.vector.scalar_tensor_tensor(out=BIAS[:, 0, :], in0=BIAS[:, 0, :], scalar=-SLOPES[0], in1=BIAS[:, 1, :],
                                                     op0=ALU.mult, op1=ALU.add))
                chain(nc.vector.scalar_tensor_tensor(out=BIAS[:, 1, :], in0=PB2[:, 0:2, :].rearrange("p s t -> p (s t)")[:, 0:896],
                                                     scalar=-SLOPES[1], in1=BIAS[:, 1, :], op0=ALU.mult, op1=ALU.add))

            def scan(i):
                n = scan_phases.index(i)
                for b in range(6):
                    chain(nc.vector.tensor_scalar(LF[:, b, :], LF[:, b, :], OMLB[:, b:b + 1], LB[:, b:b + 1], ALU.mult, ALU.add))
                    chain(nc.vector.tensor_scalar(LF[:, b, :], LF[:, b, :], TINY, None, ALU.max))
                    nc.vector.tensor_scalar(KR[:, b, :], KR[:, b, :], OMLB[:, b:b + 1], None, ALU.mult)
                    chain(nc.vector.tensor_scalar(WL[:, b, :], LF[:, b, :], SPLIT, 1.0, ALU.mult, ALU.min))
                    chain(nc.vector.tensor_scalar(LF[:, b, :], LF[:, b, :], 1.0 / SPLIT, None, ALU.max))
                    dve.drain().then_inc(gate_clamped, 1)
                chain(nc.vector.memset(E[:, :, :, 0:1], 0.0))
                for b in range(6):
                    dve.wait_ge(log_ready, 6 * n + b + 1)
                    chain(nc.vector.tensor_tensor(LF[:, b, :], LF[:, b, :], WL[:, b, :], ALU.add))
                    for t in range(4):
                        nc.vector.tensor_tensor_scan(E[:, b, t, 1:129], ONE1, LF[:, b, t * P:(t + 1) * P], 0.0, ALU.mult, ALU.add)
                dve.drain().then_inc(dve_chain, 1)
                chain.n += 1
                dve.wait_ge(dve_chain, chain.n)
                for b in range(3):
                    if 3 * n + b >= 1:
                        if b >= 1:
                            dve.wait_ge(so_ready, 6 * n + 2 * b)
                    ef, eb = E[:, b], E[:, 3 + b]
                    for d in range(2):
                        src = ef[:, :, 1:129] if d == 0 else eb[:, :, 0:128]
                        e = ef if d == 0 else eb
                        for li, m in enumerate(LEVELS):
                            w = WL[:, 7 * d + li, :].rearrange("p (t b x m) -> p t x b m", t=4, x=2, m=m)
                            x = src.rearrange("p t (b x m) -> p t x b m", x=2, m=m)
                            nb = 64 // m
                            bd = e[:, :, m:129:2 * m] if m < 64 else e[:, :, 64:65]
                            bd = bd[:, :, 0:nb]
                            for hf in range(2):
                                ins = [x[:, :, hf], bd.unsqueeze(3).broadcast_to([P, 4, nb, m])]
                                if hf == 0:
                                    ins = ins[::-1]
                                nc.vector.tensor_tensor(w[:, :, hf], ins[0], ins[1], ALU.subtract)
                    qf = QF[:].rearrange("p v (t k) -> p v t k", t=4)
                    kf = KF[:].rearrange("p v (t k) -> p v t k", t=4)
                    nc.vector.tensor_copy(qf[:, 0], ef[:, :, 1:129])
                    nc.vector.tensor_tensor(kf[:, 0], ef[:, :, 128:129].broadcast_to([P, 4, P]), ef[:, :, 1:129], ALU.subtract)
                    nc.vector.tensor_tensor(qf[:, 1], eb[:, :, 128:129].broadcast_to([P, 4, P]), eb[:, :, 0:128], ALU.subtract)
                    nc.vector.tensor_copy(kf[:, 1], eb[:, :, 0:128])
                    for d, e in enumerate((ef, eb)):
                        nc.vector.tensor_copy(ET[:, 3 * d:3 * d + 1], e[:, 1, 128:129])
                        nc.vector.tensor_copy(ET[:, 3 * d + 1:3 * d + 2], e[:, 2, 128:129])
                        nc.vector.tensor_tensor(ET[:, 3 * d + 2:3 * d + 3], e[:, 1, 128:129], e[:, 2, 128:129], ALU.add)
                    nc.vector.tensor_tensor(KS[:], KR[:, b, :], KR[:, 3 + b, :], ALU.add)
                    dve.drain().then_inc(diff_ready, 1)
                    dve.wait_ge(decay_ready, 3 * n + b + 1)
                    for d in range(2):
                        nc.vector.tensor_tensor(QF[:, d, :], QF[:, d, :], QR[:, b, :], ALU.mult)
                        nc.vector.tensor_tensor(KF[:, d, :], KF[:, d, :], KR[:, 3 * d + b, :], ALU.mult)
                    dve.drain().then_inc(dve_chain, 1)
                    chain.n += 1
                    dve.wait_ge(dve_chain, chain.n)
                    for x, (d, t, e) in enumerate(((0, 2, 0), (0, 3, 1), (0, 3, 2), (1, 0, 3), (1, 1, 4), (1, 0, 5))):
                        nc.vector.tensor_scalar(QX[:, x, :], QF[:, d, t * P:(t + 1) * P], ET[:, e:e + 1], None, ALU.mult)
                    dve.drain().then_inc(cross_ready, 1)
                    for d in range(2):
                        for li, m in enumerate(LEVELS):
                            w = WL[:, 7 * d + li, :].rearrange("p (g x m) -> p x g m", x=2, m=m)
                            q = QR[:, b, :].rearrange("p (g x m) -> p x g m", x=2, m=m)
                            k = KR[:, 3 * d + b, :].rearrange("p (g x m) -> p x g m", x=2, m=m)
                            nc.vector.tensor_tensor(w[:, 1 - d], w[:, 1 - d], q[:, 1 - d], ALU.mult)
                            nc.vector.tensor_tensor(w[:, d], w[:, d], k[:, d], ALU.mult)
                    dve.drain().then_inc(levels_ready, 1)
                    for h in (2 * b, 2 * b + 1):
                        hh = 6 * n + h
                        dve.wait_ge(pair_taken, 4 * hh + 4)
                        for dl in range(14):
                            d, li = dl // 7, dl % 7
                            m = LEVELS[li]
                            dve.wait_ge(level_ready, 14 * hh + dl + 1)
                            if 14 * hh + dl >= 1:
                                dve.wait_ge(level_taken, 14 * hh + dl)
                            nb = 64 // m
                            dst = AMD.rearrange("p t (b x m) -> p t x b m", x=2, m=m)[:, :, 1 - d]
                            mask = LEVM.bitcast(I32)[:, d, li, :].rearrange("p (b m) -> p b m", m=m).unsqueeze(1).broadcast_to([P, 4, nb, m])
                            src = ps[:, 2 + dl % 2, 0:256].rearrange("p (t b m) -> p t b m", t=4, m=m)
                            nc.vector.copy_predicated(dst, mask, src).then_inc(level_taken, 1)
                        dve.wait_ge(sosq_ready, hh + 1)
                        nc.vector.reduce_sum(small[:, 24:28], SQR.rearrange("p (t v) -> p t v", t=4), AX_X).then_inc(sor_ready, 1)
                        dve.wait_ge(so_inv, hh + 1)
                        if h % 2 == 0 and 3 * n + b >= 1:
                            dve.wait_ge(syt_ready, 3 * n + b)
                        for t in range(4):
                            x = nc.vector.tensor_scalar(SO[:, t, 64 * (h % 2):64 * (h % 2) + 64], ps[:, 4, t * 64:(t + 1) * 64],
                                                        small[:, 36 + t:37 + t], None, ALU.mult)
                        x.then_inc(so_taken, 1)
                        dve.drain().then_inc(sy_ready, 1)
                    dve.wait_ge(syt_ready, 3 * n + b + 1)
                    nc.vector.scalar_tensor_tensor(out=H[:, 5 + b, 0:S], in0=ps[:, 5, :], scalar=RNW[:, b:b + 1], in1=GR[:, b, :],
                                                   op0=ALU.mult, op1=ALU.mult).then_inc(syt_taken, 1)

            nc.vector.memset(ones[:], 1.0 / D)
            nc.vector.memset(ones4[:], 1.0 / 256)
            nc.vector.memset(small[:, 40:41], EPS)
            dve.wait_ge(consts_in, N_CONST)
            dve.wait_ge(sig_ready, 1)
            nc.vector.tensor_tensor(csil[:], cond[:], sg[:], ALU.mult)
            dve.drain().then_inc(cond_ready, 1)
            dve.drain().then_inc(setup_done, 1)
            for i, ph in enumerate(PHASES):
                kind, layer = ph["kind"], ph["layer"]
                if i in first_loads:
                    dve.wait_ge(layer_in, loads_until(i))
                if i == first0:
                    bias0()
                if i == first1:
                    lam1()
                if i in first23:
                    bounds(first23.index(i))
                    nc.vector.memset(AP_[:, :, 0:PAD], 0.0)
                    nc.vector.memset(AP_[:, :, PAD + S:], 0.0)
                    nc.vector.memset(ONE1, 1.0)
                if i in att23:
                    bias2()
                if kind == "ada":
                    w = ph["groups"][0].extra
                    dve.wait_ge(chunk_done, ph["groups"][-1].done)
                    acc = ps[:, 0, 0:48 * w].rearrange("p (n s) -> p n s", s=w)
                    for s in range(w):
                        x = nc.vector.tensor_tensor(mod[:, layer, :, s], acc[:, :, s], adab[:, layer, :], ALU.add)
                    x.then_inc(ada_taken, 1)
                    dve.wait_ge(ada_taken, layer + 1)
                    for k, o in enumerate((SC1, SC2)):
                        for s in range(w):
                            nc.vector.scalar_tensor_tensor(out=gs[:, layer, k, :, s], in0=mod[:, layer, o:o + KT, s], scalar=1.0,
                                                           in1=gvec[:, layer, k, :], op0=ALU.add, op1=ALU.mult)
                elif kind in ("norm", "final"):
                    norm(i, ph, kind == "final")
                elif kind == "linear":
                    for g in ph["groups"]:
                        if g.by in ("dve", "act+dve") or g.role.startswith("rope"):
                            take(g)
                elif kind == "attention":
                    attention(layer)
                elif kind == "conv":
                    conv(i)
                elif kind == "scan":
                    scan(i)
                end_phase(dve, i)

        @block.gpsimd
        def _(pool):
            def load(dst, src, s):
                nc.gpsimd.dma_start(dst, src).then_inc(s, 16)

            steps = [0]

            def inverse_root(dst, src):
                steps[0] += 1
                nc.gpsimd.tensor_scalar(src, src, EPS, None, ALU.add).then_inc(pool_step, 1)
                pool.wait_ge(pool_step, steps[0])
                return nc.gpsimd.tensor_tensor(dst, src, small[:, 44:44 + dst.shape[1]], ALU.pow)

            def layer_loads(i):
                if i == first0:
                    load(COS, a["cos"], layer_in)
                    load(SIN, a["sin"], layer_in)
                    load(WIN, a["win"], layer_in)
                    load(SINK, a["sink"], layer_in)
                    load(NA, a["na"], layer_in)
                    for r in range(ROWS):
                        src = bass.AP(a["rpb"].tensor, 31 * r, [[1, 16], [15 * 31, 8], [1, 265]])
                        load(RPBW[16 * r:16 * r + 16], src, layer_in)
                if i == first1:
                    load(COS, a["cos"], layer_in)
                    load(SIN, a["sin"], layer_in)
                    load(SUBG, a["subg"], layer_in)
                    load(LAMV, a["lam"], layer_in)
                if i in first23:
                    k = first23.index(i)
                    load(LEVM.bitcast(I32), a["lev"], layer_in)
                    load(CAW, a["caw"][k], layer_in)
                    load(CAV, a["cav"][k], layer_in)
                    load(GAM, a["gam"], layer_in)
                    load(RNW, a["rnw"][k], layer_in)
                if i in up23:
                    load(CFW, a["cfw"][up23.index(i)], layer_in)
                if i in att23:
                    load(BIAS[:, 0, :], a["dist"], layer_in)
                    load(BIAS[:, 1, :], a["logc"], layer_in)

            def root(j):
                pool.wait_ge(o_squares, j + 1)
                inverse_root(small[:, 24 + j % 2:25 + j % 2], small[:, 20 + j % 2:21 + j % 2]).then_inc(o_inv, 1)

            nc.gpsimd.memset(small[:, 44:48], -0.5).then_inc(pool_step, 1)
            steps[0] = 1
            pool.wait_ge(pool_step, 1)
            for i, ph in enumerate(PHASES):
                kind, layer = ph["kind"], ph["layer"]
                if i in first_loads:
                    layer_loads(i)
                if kind == "linear":
                    for g in ph["groups"]:
                        if g.role.startswith("rope"):
                            n = rope_groups.index(g)
                            pool.wait_ge(rot_ready, n + 1)
                            r = ROTB[:, n % 2, 0:S]
                            nc.gpsimd.tensor_tensor(r, r, SIN, ALU.mult).then_inc(rot_scaled, 1)
                        elif g.role == "relu":
                            n = relu_groups.index(g)
                            pool.wait_ge(relu_ready, n + 1)
                            hb = HID1[:, g.index, 0:g.cols]
                            nc.gpsimd.tensor_tensor(hb, hb, hb, ALU.mult)
                        elif g.role == "ffn_val":
                            n = ffn_groups.index(g) // 2
                            pool.wait_ge(gelu_ready, n + 1)
                            pool.wait_ge(conv_out, 2 * n + 2)
                            nc.gpsimd.tensor_tensor(HID[:, g.index, :], GL[:, n % 2, :], UV[:, n % 2, :], ALU.mult).then_inc(hid_ready, 1)
                elif kind == "attention" and layer == 1:
                    for j in range(len(value_items(1))):
                        pool.wait_ge(inv_ready, att_base[1] + 2 * j + 2)
                        i1 = 2 * j + 1
                        second = PB[:, 2 * (j % 2) + 1, 0:T]
                        nc.gpsimd.tensor_scalar(second, second, small[:, 12 + i1 % 4:13 + i1 % 4], None,
                                                ALU.mult).then_inc(second_scaled, 1)
                        if j >= 2:
                            root(j - 2)
                    root(len(value_items(1)) - 2)
                    root(len(value_items(1)) - 1)
                elif kind == "scan":
                    n = scan_phases.index(i)
                    for hh in range(6 * n, 6 * n + 6):
                        pool.wait_ge(sor_ready, hh + 1)
                        inverse_root(small[:, 36:40], small[:, 24:28]).then_inc(so_inv, 1)
                end_phase(pool, i)



def tiles(w):
    k, n = w.shape
    return np.ascontiguousarray(w.reshape(k // P, P, n // P, P).transpose(2, 1, 0, 3))


def columns(v):
    return v.reshape(-1, P).T


def even_order():
    cols = []
    for base in (0, 768):
        for b in range(4):
            for h in (b, b + 4):
                cols += range(base + 64 * h, base + 64 * h + 64)
        cols += range(base + 512, base + 768)
    return np.array(cols)


def kernel(**inputs):
    import concourse.bacc as bacc
    from concourse.bass_utils import run_bass_kernel_spmd

    x = {k: np.asarray(v) for k, v in inputs.items()}
    arrays = {}
    arrays["xT"] = np.concatenate([x["x"][0], x["ctx"][0]], 0).T.reshape(KT, P, T)
    arrays["cond"] = np.stack([columns(x["c"][0]), columns(x["c_ctx"]), columns(x["c_2"][0])], 1)
    arrays["ada_b"] = np.stack([columns(b) for b in (*x["ada_b"], *x["b_ada_2"])], 1)
    arrays["norm_g"] = np.stack([np.stack([columns(g1), columns(g2)], 1)
                                 for g1, g2 in [*zip(x["norm1_g"], x["norm2_g"]), *zip(x["norm1_w_2"], x["norm2_w_2"])]], 1)
    arrays["fin_g"] = np.stack([columns(x["final_g"]), columns(x["final_norm_w_2"])], 1)
    for layer in range(2):
        arrays[f"ada{layer}"] = tiles(x["ada_w"][layer])
        arrays[f"ada{layer + 2}"] = tiles(x["w_ada_2"][layer])
        arrays[f"mlp1_{layer}"] = tiles(x["mlp_w1"][layer])
        arrays[f"mlp2_{layer}"] = tiles(x["mlp_w2"][layer])
        arrays[f"in{layer + 2}"] = tiles(x["w_in_2"][layer])
        arrays[f"out{layer + 2}"] = tiles(x["w_out_2"][layer])
        arrays[f"up{layer + 2}"] = tiles(x["w_up_2"][layer])
        arrays[f"down{layer + 2}"] = tiles(x["w_down_2"][layer])
    arrays["even_in"] = tiles(x["even_w_in"][0][:, even_order()])
    arrays["odd_in"] = tiles(x["odd_w_in"][0])
    arrays["out0"] = tiles(x["even_w_out"][0])
    arrays["out1"] = tiles(x["odd_w_out"][0])
    arrays["sink"] = np.broadcast_to(x["a_sink"][0][None], (P, 8))
    arrays["rpb"] = np.pad(x["b_rpb"][0][:, ::-1, ::-1].reshape(-1), (16, 32))
    arrays["subg"] = x["subln_g"][0].reshape(P, 1)
    arrays["lam"] = np.broadcast_to(np.stack([x[k][0] for k in ("lam_q1", "lam_k1", "lam_q2", "lam_k2")])[None], (P, 4, DH))
    arrays["caw"] = x["conv_a_w_2"].transpose(0, 2, 1).reshape(2, 2, P, CONV).transpose(0, 2, 1, 3)
    arrays["cav"] = np.stack([x[k].reshape(2, 2, P) for k in ("conv_a_b_2", "ln_a_w_2", "ln_a_b_2")], -1).transpose(0, 2, 1, 3)
    arrays["gam"] = x["lb_gamma_2"].reshape(2, 2, 3, P).transpose(3, 0, 1, 2)
    arrays["rnw"] = x["rec_norm_w_2"].reshape(2, 3, P).transpose(0, 2, 1)
    arrays["cfw"] = x["conv_f_w_2"].transpose(0, 2, 1).reshape(2, 2 * NB2, P, 3).transpose(0, 2, 1, 3)
    for k, v in constants().items():
        arrays[k] = v.astype(np.int32 if k == "lev" else np.float32)
    arrays = {"in_" + k: np.ascontiguousarray(v) for k, v in arrays.items()}

    nc = bacc.Bacc("TRN2", target_bir_lowering=False, num_devices=1)
    args = {k[3:]: nc.dram_tensor(k, v.shape, mybir.dt.from_np(v.dtype), kind="ExternalInput").ap() for k, v in arrays.items()}
    out = nc.dram_tensor("outT", (KT, P, S), F32, kind="ExternalOutput").ap()
    build(nc, args, out)
    got = run_bass_kernel_spmd(nc, [arrays], core_ids=[0]).results[0]["outT"]
    return np.ascontiguousarray(np.asarray(got).reshape(D, S).T).reshape(1, S, D)
```

```python
import math
from contextlib import ExitStack

import numpy as np

import concourse.bass as bass
from concourse import mybir

F32 = mybir.dt.float32
I32 = mybir.dt.int32
ALU = mybir.AluOpType
ACT = mybir.ActivationFunctionType
AX_X = mybir.AxisListType.X

P = 128
D = 1024
KT = D // P
S = 512
C = 256
T = S + C
DH = 64
GRID = 64
ROWS = S // GRID
DFF = 4 * D
HALF = DFF // 2 // P
DFF2 = 2816
NB2 = DFF2 // P
EPS = 1e-6
NEG = -1e30
LAM_INIT = 0.8 - 0.6 * math.exp(-0.3)
TINY = 1e-30
SPLIT = 2.0 ** 60
CONV = 31
PAD = CONV // 2
RING = 4
ARENA_F = 27200 + 300
ARING = 2
NSLOT = 4
ROT = list(range(16, 32)) + list(range(16))
LEVELS = [1, 2, 4, 8, 16, 32, 64]

SH1, SC1, G1, SH2, SC2, G2 = (i * KT for i in range(6))



class Group:

    def __init__(self, form, weight, chunks, by, role, index, source="h", cols=None, extra=None):
        self.form, self.weight, self.by, self.role, self.index = form, weight, by, role, index
        self.chunks = chunks
        self.source, self.cols, self.extra = source, cols, extra
        self.n = self.first = None

    @property
    def slot(self):
        return self.n % NSLOT

    @property
    def freed_before(self):
        return self.n // NSLOT

    @property
    def done(self):
        return self.first + len(self.chunks)


def full(nb):
    return [(nb, 0, KT)]


def plan():
    phases = []

    def add(kind, layer, groups=(), **more):
        phases.append(dict(kind=kind, layer=layer, groups=list(groups), **more))

    add("ada", 0)
    for layer in range(2):
        add("norm", layer, which=1, cols=T)
        if layer == 0:
            g = [Group("feat", "even_in", full(nb), "act", "rope_q", nb, cols=T) for nb in range(4)]
            g += [Group("feat", "even_in", full(4), "act", "rope_k", 0, cols=T)]
            g += [Group("tok", "even_in", full(5), "act", "va", 0)]
            g += [Group("feat", "even_in", full(6 + nb), "dve", "plain_q", 4 + nb, cols=T) for nb in range(4)]
            g += [Group("feat", "even_in", full(10), "dve", "plain_k", 1, cols=T)]
            g += [Group("feat", "even_in", full(11), "act", "vbt", 0, cols=T)]
            g += [Group("turn", "even_in", [], "act", "vb", j) for j in range(2)]
        else:
            g = [Group("feat", "odd_in", full(nb), "act", "rope_q", nb, cols=S) for nb in range(8)]
            g += [Group("feat", "odd_in", full(8 + nb), "act", "rope_k", nb, cols=T) for nb in range(8)]
            g += [Group("tok", "odd_in", full(16 + nb), "dve", "v1", nb) for nb in range(8)]
        add("linear", layer, g)
        add("attention", layer)
        cols = T if layer == 0 else S
        add("linear", layer, [Group("feat", f"out{layer}", full(nb), "dve", "residual", nb, source="y", cols=cols, extra=G1)
                              for nb in range(KT)])
        add("norm", layer, which=2, cols=cols)
        g = []
        for half in range(2):
            g += [Group("feat", f"mlp1_{layer}", full(half * HALF + j), "act", "relu", j, cols=cols) for j in range(HALF)]
            g += [Group("feat", f"mlp2_{layer}", [(nb, half * HALF, KT), (nb, half * HALF + KT, KT)],
                        "dve", "residual", nb, source="hid", cols=cols, extra=G2) for nb in range(KT)]
        add("linear", layer, g)
    add("final", 0)
    for layer in (2, 3):
        add("norm", layer, which=1, cols=S)
        w = f"in{layer}"
        g = []
        for j in range(2):
            g += [Group("feat", w, full(2 + j), "act", "gate_a", j, cols=S), Group("feat", w, full(j), "dve", "val_a", j, cols=S)]
        g += [Group("feat", w, full(4 + j), "act", "q2", j, cols=S) for j in range(3)]
        g += [Group("feat", w, full(7 + j), "dve", "k2", j, cols=S) for j in range(3)]
        g += [Group("tok", w, full(10 + j), "act", "v2", j, cols=S) for j in range(3)]
        g += [Group("feat", w, full(13 + j), "act", "silu_q", j, cols=S) for j in range(3)]
        g += [Group("feat", w, full(25 + j), "act", "silu_g", j, cols=S) for j in range(3)]
        g += [Group("feat", w, full(16 + j), "act", "z", j, cols=S) for j in range(6)]
        g += [Group("tok", w, full(22 + j), "dve", "vr", j, cols=S) for j in range(3)]
        add("linear", layer, g)
        add("conv", layer)
        add("attention", layer)
        add("scan", layer)
        add("linear", layer, [Group("feat", f"out{layer}", full(nb), "dve", "residual", nb, source="y", cols=S, extra=G1)
                              for nb in range(KT)])
        add("norm", layer, which=2, cols=S)
        g = []
        for j in range(NB2):
            g += [Group("feat", f"up{layer}", full(j), "act+dve", "ffn_gate", j, cols=S),
                  Group("feat", f"up{layer}", full(NB2 + j), "act+dve", "ffn_val", j, cols=S)]
        g += [Group("feat", f"down{layer}", [(nb, 0, 8), (nb, 8, 8), (nb, 16, 6)],
                    "dve", "residual", nb, source="hid", cols=S, extra=G2) for nb in range(KT)]
        add("linear", layer, g)
    add("final", 1)
    chunks, n = [], 0
    for ph in phases:
        for g in ph["groups"]:
            g.first = len(chunks)
            chunks += [(g.weight, *c) for c in g.chunks]
            g.n = n
            n += 1
    return phases, chunks


def modulation_plan(phases):
    linear = [[i for i, ph in enumerate(phases) if ph["kind"] == "linear" and ph["layer"] == layer] for layer in range(4)]
    mlp = {layer: linear[layer][2:] for layer in range(4)}
    found = {0: [(0, nb, 2) for nb in range(2 * KT)], linear[0][0]: [(0, nb, 2) for nb in range(2 * KT, 6 * KT)]}

    def spread(items, over):
        for n, i in enumerate(over):
            found[i] = items[n * len(items) // len(over):(n + 1) * len(items) // len(over)]

    spread([(1, nb, 2 if nb < 2 * KT else 1) for nb in range(6 * KT)], mlp[0])
    spread([(2, nb, 1) for nb in range(6 * KT)], mlp[1])
    spread([(3, nb, 1) for nb in range(6 * KT)], mlp[2])
    return found


def attention_items(layer):
    if layer == 0:
        return ([("a", h, n) for n in range(4) for h in range(8)] + [("b", h, m) for m in range(4) for h in range(8)]
                + [("ca", h, n) for n in range(2) for h in range(8)] + [("cb", h, n) for n in range(2) for h in range(8)])
    if layer == 1:
        return [("d", h, n, m) for n in range(4) for h in range(8) for m in range(2)]
    return [("e", h, n) for n in range(4) for h in range(6)]



def constants():
    t = np.arange(S)
    row, col = (t // GRID).astype(np.float32), (t % GRID).astype(np.float32)
    quarter = DH // 4
    inv = (np.float32(10000.0) ** (-np.arange(quarter, dtype=np.float32) / quarter)).astype(np.float32)
    ar, ac = row[:, None] * inv[None], col[:, None] * inv[None]
    ang = np.concatenate([ar, ar, ac, ac], -1)
    sign = np.where((np.arange(DH) % 32) < 16, -1.0, 1.0)
    cos = np.tile(np.cos(ang).T, (2, 1))
    sin = np.tile((np.sin(ang) * sign).T, (2, 1))
    p, f = np.arange(P)[:, None], np.arange(P)[None]
    win = np.stack([np.where(f >= p, 0.0, NEG), np.where(f <= p, 0.0, NEG)], 1)
    na = np.zeros((P, 3, ROWS, 32), np.float32)
    for v, m in enumerate((0, 1, 3)):
        qc = m * 16 + (np.arange(P) % 16)
        kc = min(max(m * 16 - 8, 0), 32) + np.arange(32)
        cs = np.clip(qc - 8, 0, GRID - 16)
        ok = (kc[None] >= cs[:, None]) & (kc[None] < cs[:, None] + 16)
        na[:, v] = np.where(ok, 0.0, NEG)[:, None, :]
    u = np.arange(896)[None]
    rel = np.abs(p - u + 384)
    count = (rel <= 64).astype(int) + ((rel % 4 == 0) & (rel // 4 <= 64)) + ((rel % 16 == 0) & (rel // 16 <= 64))
    logc = np.where(count > 0, np.log(np.maximum(count, 1)), NEG)
    lev = np.zeros((P, 2, len(LEVELS), 64), np.int32)
    for li, m in enumerate(LEVELS):
        for x in range(64):
            blk = x // m
            s = np.arange(P)
            lev[:, 0, li, x] = (s // (2 * m) == blk) & (s % (2 * m) < m)
            lev[:, 1, li, x] = (s // (2 * m) == blk) & (s % (2 * m) >= m)
    return dict(cos=cos, sin=sin, win=win, na=na.reshape(P, 3, 256), dist=rel * np.ones((P, 1)), logc=logc * np.ones((P, 1)),
                lev=lev, ident=np.eye(P))


SLOPES = [2.0 ** (-8.0 * i / 6) for i in range(1, 7)]


def build(nc, a, out):
    PHASES, CHUNKS = plan()
    with ExitStack() as ctx:
        def sb(name, shape, dt=F32):
            return ctx.enter_context(nc.sbuf_tensor(name, shape, dt))

        def sem(name):
            return ctx.enter_context(nc.semaphore(name))

        ps = ctx.enter_context(nc.psum_tensor("ps", [P, 8, 512], F32))
        psf = ps[:, :, :].rearrange("p b n -> p (b n)")

        ring = sb("ring", [P, RING, KT, P])
        X = sb("resid", [P, KT, T])
        H = sb("hbuf", [P, KT, T])
        ARENA = sb("arena", [P, ARENA_F])
        JUNK = sb("junk", [P, D])
        X_SG = ARENA[:, 0:2 * D].rearrange("p (s d) -> p s d", s=2)
        ones = sb("ones", [P, P])
        ones4 = sb("ones4", [P, P])
        ident = sb("ident", [P, P])
        R = sb("rstd", [P, T])
        mod = sb("mod", [P, 4, 48, 2])
        gs = sb("gs", [P, 4, 2, KT, 2])
        adab = sb("adab", [P, 4, 48])
        gvec = sb("gvec", [P, 4, 2, KT])
        fin_g = sb("fin_g", [P, 2, KT])
        csil = sb("csil", [P, 2, D])
        aring = sb("aring", [P, ARING, D])
        small = sb("small", [P, 64])

        off = [0]

        def carve(n, pattern=None, **k):
            v = ARENA[:, off[0]:off[0] + n]
            off[0] += n
            assert off[0] <= ARENA_F, off[0]
            return v.rearrange(pattern, **k) if pattern else v

        off[0] = 0
        QT = carve(8 * T, "p (b t) -> p b t", b=8)
        KTT = carve(8 * T, "p (b t) -> p b t", b=8)
        VV = carve(6 * 1024, "p (t v) -> p t v", t=6)
        mark = off[0]
        PB = carve(4 * T, "p (s t) -> p s t", s=4)
        PT = carve(2 * T, "p (s t) -> p s t", s=2)
        YT = carve(2 * P, "p (s t) -> p s t", s=2)
        ROTB = PB
        VBT = PB.rearrange("p s t -> p (s t)")[:, 2 * T:2 * T + 1280]
        base_small = off[0]
        off[0] = 8 * T + 2 * T
        BM = carve(8 * 3 * 256, "p (h v k) -> p h v k", h=8, v=3)
        off[0] = base_small
        COS = carve(S)
        SIN = carve(S)
        WIN = carve(2 * P, "p (v k) -> p v k", v=2)
        SINK = carve(8)
        SUBG = carve(1)
        LAMV = carve(4 * DH, "p (v k) -> p v k", v=4)
        LAMS = carve(8)
        SUBT = carve(P)
        QB1 = carve(8 * 2 * P, "p (b t) -> p b t", b=8)
        after_att = off[0]
        KP1 = ARENA[:, 15872:15872 + 2 * T].rearrange("p (b t) -> p b t", b=2)
        V0 = ARENA[:, 8 * T + 2 * T + 6144:8 * T + 2 * T + 6144 + 16 * P].rearrange("p (t v) -> p t v", t=16)
        assert 8 * T + 2 * T + 6144 + 16 * P <= mark
        off[0] = 0
        NA = carve(3 * 256, "p (v k) -> p v k", v=3)
        RPBW = carve(8 * 265, "p (h k) -> p h k", h=8)
        off[0] = 0
        HID = carve(NB2 * S, "p (b t) -> p b t", b=NB2)
        HID1 = ARENA[:, 0:HALF * T].rearrange("p (b t) -> p b t", b=HALF)
        off[0] = max(HALF * T, NB2 * S)
        UG = carve(2 * S, "p (s t) -> p s t", s=2)
        UV = carve(2 * S, "p (s t) -> p s t", s=2)
        CFW = carve(3 * 2 * NB2, "p (b k) -> p b k", k=3)
        GL = carve(2 * S, "p (s t) -> p s t", s=2)
        off[0] = 0
        Q2 = carve(3 * S, "p (b t) -> p b t", b=3)
        K2 = carve(3 * S, "p (b t) -> p b t", b=3)
        V2 = carve(4 * 384, "p (t v) -> p t v", t=4)
        QR = carve(3 * S, "p (b t) -> p b t", b=3)
        GR = carve(3 * S, "p (b t) -> p b t", b=3)
        VR = carve(4 * 384, "p (t v) -> p t v", t=4)
        KR = carve(6 * S, "p (b t) -> p b t", b=6)
        LF = carve(6 * S, "p (b t) -> p b t", b=6)
        at_conv = off[0]
        SGA = carve(2 * S, "p (b t) -> p b t", b=2)
        AP_ = carve(2 * (S + 2 * PAD), "p (b t) -> p b t", b=2)
        AC = carve(2 * S, "p (b t) -> p b t", b=2)
        AQ = carve(2 * S, "p (b t) -> p b t", b=2)
        at_att2 = off[0]
        off[0] = at_conv
        BIAS = carve(6 * 896, "p (h k) -> p h k", h=6)
        PB2 = carve(2 * T, "p (s t) -> p s t", s=2)
        PT2 = carve(2 * T, "p (s t) -> p s t", s=2)
        YT2 = carve(2 * P, "p (s t) -> p s t", s=2)
        end1 = off[0]
        off[0] = at_att2
        LTMP = carve(6 * S, "p (b t) -> p b t", b=6)
        off[0] = at_conv - 6 * S
        WL = carve(14 * S, "p (v t) -> p v t", v=14)
        E = carve(6 * 4 * 129, "p (b t k) -> p b t k", b=6, t=4)
        QF = carve(2 * S, "p (v t) -> p v t", v=2)
        KF = carve(2 * S, "p (v t) -> p v t", v=2)
        QX = carve(6 * P, "p (v t) -> p v t", v=6)
        KS = carve(S)
        ET = carve(6)
        SO = JUNK[:, 0:S].rearrange("p (t v) -> p t v", t=4)
        end2 = off[0]
        AM = ARENA[:, 0:8 * S].rearrange("p (h j t) -> p h j t", h=2, j=4)
        SQR = ARENA[:, 8 * S:8 * S + 512].rearrange("p (h v) -> p h v", h=2)
        SO_BANK = (4, 6)

        def level_queries(v):
            k = v % 8
            return (X, H)[k // 4][:, 2 * (k % 4):2 * (k % 4) + 2, S:T]

        def own_values(hx):
            return ps[:, SO_BANK[hx], :].rearrange("p (t v) -> p t v", t=4)[:, :, 64 * hx:64 * hx + 64]

        def diagonal(hx):
            return ARENA[:, 4 * S * hx:4 * S * hx + 5 * S].rearrange("p (t r) -> p t r", r=S + P)[:, :, 0:P]

        off[0] = max(end1, end2, at_att2)
        LEVM = carve(14 * 64, "p (d l k) -> p d l k", d=2, l=7)
        CAW = carve(2 * CONV, "p (b k) -> p b k", b=2)
        CAV = carve(6, "p (b k) -> p b k", b=2)
        GAM = carve(12, "p (d l b) -> p d l b", d=2, l=2)
        LB = carve(6)
        OMLB = carve(6)
        GTMP = carve(24, "p (k b) -> p k b", k=4)
        RNW = carve(3)
        ONE1 = carve(P)

        consts_in = sem("consts_in")
        late_in = sem("late_in")
        w_arrived = [sem(f"w_arrived{i}") for i in range(RING)]
        chunk_done = sem("chunk_done")
        group_freed = [sem(f"group_freed{i}") for i in range(NSLOT)]
        phase_done = sem("phase_done")
        act_chain = sem("act_chain")
        dve_chain = sem("dve_chain")
        pool_chain = sem("pool_chain")
        setup_done = sem("setup_done")
        ada_arrived = [sem(f"ada_arrived{i}") for i in range(ARING)]
        ada_used = sem("ada_used")
        ada_first = sem("ada_first")
        cond2_in = sem("cond2_in")
        cond2_sig = sem("cond2_sig")
        sq_ready = sem("sq_ready")
        stats_ready = sem("stats_ready")
        rstd_ready = sem("rstd_ready")
        scaled_ready = sem("scaled_ready")
        rope_in = sem("rope_in")
        rot_ready = sem("rot_ready")
        rot_scaled = sem("rot_scaled")
        relu_ready = sem("relu_ready")
        scores_ready = sem("scores_ready")
        max_ready = sem("max_ready")
        probs_ready = sem("probs_ready")
        probs_mixed = sem("probs_mixed")
        inv_ready = sem("inv_ready")
        pt_ready = sem("pt_ready")
        pt_copied_act = sem("pt_copied_act")
        pt_copied_dve = sem("pt_copied_dve")
        o_ready = sem("o_ready")
        y_ready = sem("y_ready")
        yt_ready = sem("yt_ready")
        yt_taken = sem("yt_taken")
        conv_first = sem("conv_first")
        conv_out = sem("conv_out")
        gelu_ready = sem("gelu_ready")
        hid_ready = sem("hid_ready")
        sig_ready = sem("sig_ready")
        conv_ready = sem("conv_ready")
        ln_step = sem("ln_step")
        ln_mean = sem("ln_mean")
        ln_x = sem("ln_x")
        diff_ready = sem("diff_ready")
        decay_ready = sem("decay_ready")
        unit_ready = sem("unit_ready")
        query_ready = sem("query_ready")
        pair_ready = sem("pair_ready")
        pair_taken = sem("pair_taken")
        level_ready = sem("level_ready")
        level_taken = sem("level_taken")
        so_ready = sem("so_ready")
        so_taken = sem("so_taken")
        sosq_ready = sem("sosq_ready")
        sor_ready = sem("sor_ready")
        sy_ready = sem("sy_ready")
        syt_ready = sem("syt_ready")
        syt_taken = sem("syt_taken")
        out_ready = sem("out_ready")
        out_stored = sem("out_stored")
        layer_in = sem("layer_in")
        vbt_ready = sem("vbt_ready")
        vb_turned = sem("vb_turned")
        root_scale = sem("root_scale")
        squared = sem("squared")
        lam_sums = sem("lam_sums")
        lam_exp = sem("lam_exp")
        gam_ready = sem("gam_ready")
        gam_exp = sem("gam_exp")
        o_squares = sem("o_squares")
        o_inv = sem("o_inv")
        so_inv = sem("so_inv")
        gate_clamped = sem("gate_clamped")
        z_ready = sem("z_ready")
        log_ready = sem("log_ready")
        pool_step = sem("pool_step")

        block = ctx.enter_context(nc.Block())

        class Chain:

            def __init__(self, eng, s):
                self.eng, self.sem, self.n = eng, s, 0

            def __call__(self, ins):
                self.n += 1
                ins.then_inc(self.sem, 1)
                self.eng.wait_ge(self.sem, self.n)

        def end_phase(eng, i):
            eng.drain().then_inc(phase_done, 1)
            eng.wait_ge(phase_done, 4 * (i + 1))

        ATT = {layer: attention_items(layer) for layer in range(4)}
        att_base, n_att = {}, 0
        for ph in PHASES:
            if ph["kind"] == "attention":
                att_base[ph["layer"]] = n_att
                n_att += len(ATT[ph["layer"]])

        def value_items(layer):
            its = ATT[layer]
            return its if layer != 1 else its[::2]

        val_base, n_val = {}, 0
        pt2_base, n_pt2 = {}, 0
        yt_base, n_yt = {}, 0

        def key_tiles(item):
            kind = item[0]
            if kind == "a":
                return 5 if 0 < item[2] < 3 else 4
            return {"b": 4, "ca": 2, "cb": 2, "d": 6, "e": 4}[kind]

        for ph in PHASES:
            if ph["kind"] == "attention":
                layer = ph["layer"]
                val_base[layer], pt2_base[layer], yt_base[layer] = n_val, n_pt2, n_yt
                n_val += len(value_items(layer))
                n_pt2 += sum(key_tiles(i) > 4 for i in value_items(layer))
                n_yt += len(value_items(layer)) // (2 if layer != 1 else 1)
        mixed_base = 0

        @block.sync
        def _(sp):
            def load(dst, src, s=consts_in):
                sp.dma_start(dst, src).then_inc(s, 16)

            load(csil[:, 0, :], a["cond"][:, 0, :])
            load(csil[:, 1, :], a["cond"][:, 1, :])
            load(adab[:], a["ada_b"])
            load(gvec[:], a["norm_g"])
            load(fin_g[:], a["fin_g"])
            load(ident[:], a["ident"])
            for kt in range(KT):
                load(X[:, kt, :], a["xT"][kt])

            def chunk(c):
                name, nb, k0, nk = CHUNKS[c]
                if c >= RING:
                    sp.wait_ge(chunk_done, c - RING + 1)
                sp.dma_start(ring[:, c % RING, 0:nk, :], a[name][nb, :, k0:k0 + nk, :]).then_inc(w_arrived[c % RING], 16)

            c = 0
            for i, ph in enumerate(PHASES):
                for g in ph["groups"]:
                    for _ in g.chunks:
                        chunk(c)
                        c += 1
            for kt in range(KT):
                sp.wait_ge(out_ready, kt + 1)
                sp.dma_start(out[kt], H[:, kt, 0:S]).then_inc(out_stored, 16)
            sp.wait_ge(out_stored, 16 * KT)

        def sources(g):
            return {"h": H, "y": H, "hid": HID1 if g.weight.startswith("mlp") else HID}[g.source]

        def product(pe, g):
            slot = psf[:, g.slot * 1024:(g.slot + 1) * 1024]
            if g.n >= NSLOT:
                pe.wait_ge(group_freed[g.slot], g.freed_before)
            src = sources(g)
            if g.form == "turn":
                pe.wait_ge(vbt_ready, 1)
                for t in range(8 * g.index, min(8 * g.index + 8, 10)):
                    mm = nc.tensor.transpose(slot[:, (t % 8) * P:(t % 8 + 1) * P], VBT[:, t * P:(t + 1) * P], ident[:, :])
                mm.then_inc(vb_turned, 1)
                return
            nkt = sum(n for _, _, n in g.chunks)
            if g.form == "feat":
                kt = 0
                for ci, (_, _, n) in enumerate(g.chunks):
                    c = g.first + ci
                    pe.wait_ge(w_arrived[c % RING], 16 * (c // RING + 1))
                    for k in range(n):
                        if g.source == "hid" and g.index == 0:
                            if g.weight.startswith("mlp"):
                                pe.wait_ge(squared, relu_groups.index(hidden_of(g, kt)) + 1)
                            else:
                                pe.wait_ge(hid_ready, ffn_groups.index(hidden_of(g, kt)) // 2 + 1)
                        for lo, hi in ((0, S), (S, T)):
                            if lo >= g.cols:
                                continue
                            mm = nc.tensor.matmul(slot[:, lo:hi], ring[:, c % RING, k, :], src[:, kt, lo:hi],
                                                  start=kt == 0, stop=kt == nkt - 1)
                        kt += 1
                    mm.then_inc(chunk_done, 1)
                return
            c = g.first
            pe.wait_ge(w_arrived[c % RING], 16 * (c // RING + 1))
            if g.form == "tok":
                tiles = [src[:, :, t * P:(t + 1) * P] for t in range((g.cols or T) // P)]
            for t, lhs in enumerate(tiles):
                for k in range(KT):
                    mm = nc.tensor.matmul(slot[:, t * P:(t + 1) * P], lhs[:, k], ring[:, c % RING, k, :],
                                          start=k == 0, stop=k == KT - 1)
            mm.then_inc(chunk_done, 1)

        def phase_index(kind, layer, nth=0):
            return [i for i, ph in enumerate(PHASES) if ph["kind"] == kind and ph["layer"] == layer][nth]

        first0 = phase_index("norm", 0)
        first1 = phase_index("norm", 1)
        first23 = [phase_index("norm", 2), phase_index("norm", 3)]
        up23 = [phase_index("norm", 2, 1), phase_index("norm", 3, 1)]
        att23 = [phase_index("attention", 2), phase_index("attention", 3)]
        cond2_phase = min(i for i, its in modulation_plan(PHASES).items() if its and its[0][0] == 2)
        first_loads = [first0, first1] + first23 + up23 + att23
        n_loads = {first0: 5 + ROWS, first1: 4, **{i: 5 for i in first23}, **{i: 1 for i in up23}, **{i: 2 for i in att23}}

        def loads_until(i):
            return 16 * sum(n for j, n in n_loads.items() if j <= i)

        N_CONST = 16 * (6 + KT)
        MOD = modulation_plan(PHASES)
        mod_items = [it for i in sorted(MOD) for it in MOD[i]]
        mod_base = {i: sum(len(MOD[j]) for j in MOD if j < i) for i in range(len(PHASES) + 1)}

        def mod_share(i, n=0, of=1):
            m = len(MOD.get(i, ()))
            return range(mod_base[i] + n * m // of, mod_base[i] + (n + 1) * m // of)

        rope_groups = [g for ph in PHASES for g in ph["groups"] if g.role.startswith("rope")]
        relu_groups = [g for ph in PHASES for g in ph["groups"] if g.role == "relu"]
        ffn_groups = [g for ph in PHASES for g in ph["groups"] if g.role.startswith("ffn")]

        def hidden_of(g, kt):
            before = [x for ph in PHASES for x in ph["groups"] if x.role in ("relu", "ffn_val") and x.first < g.first]
            return [x for x in before[-NB2:] if x.index == kt][-1]

        gate_groups = [g for ph in PHASES for g in ph["groups"] if g.role == "gate_a"]
        norm_phases = [i for i, ph in enumerate(PHASES) if ph["kind"] in ("norm", "final")]
        conv_phases = [i for i, ph in enumerate(PHASES) if ph["kind"] == "conv"]
        rstd_order = sorted(norm_phases + conv_phases)
        scaled_before = {i: KT * sum(j < i and PHASES[j]["kind"] == "norm" for j in norm_phases) for i in norm_phases}
        mixer_phases = [i - 1 for i in conv_phases]
        scan_phases = [i for i, ph in enumerate(PHASES) if ph["kind"] == "scan"]

        def ranges(cols):
            return [(0, S, 0), (S, T, 1)][:1 if cols == S else 2]

        def pieces(layer, item):
            kind, h, n = item[:3]
            if layer == 0:
                if kind in ("a", "ca"):
                    blk, kb, kv = h % 4, 0, h // 4
                else:
                    blk, kb, kv = 4 + h % 4, 1, h // 4
                q, k = QT[:, blk], (KTT, KP1)[kv][:, kb]
                vs = slice(0, P)
                if kind == "a":
                    lo, hi = max(n - 1, 0), min(n + 1, 3)
                    two = min(lo + 2, hi + 1)
                    ks = [(k[:, S:T], 0), (k[:, lo * P:two * P], C)]
                    if hi + 1 > two:
                        ks.append((k[:, hi * P:(hi + 1) * P], 512))
                    v = [V0[:, 4, vs], V0[:, 5, vs]] + [V0[:, t, vs] for t in range(lo, hi + 1)]
                    return q[:, n * P:(n + 1) * P], ks, v
                if kind == "b":
                    c0 = (0, 8, 24, 32)[n]
                    kg = k[:, 0:S].rearrange("p (r c) -> p r c", c=GRID)[:, :, c0:c0 + 32]
                    v = [V0[:, 6 + 2 * n, vs], V0[:, 7 + 2 * n, vs], V0[:, 14, vs], V0[:, 15, vs]]
                    return q[:, n * P:(n + 1) * P], [(kg, 0), (k[:, S:T], C)], v
                vt = (4, 5) if kind == "ca" else (14, 15)
                return q[:, S + n * P:S + (n + 1) * P], [(k[:, S:T], 0)], [V0[:, t, vs] for t in vt]
            if layer == 1:
                m = item[3]
                k = KTT[:, h]
                if m == 0:
                    q = QT[:, h, n * P:(n + 1) * P]
                else:
                    q = (QT[:, h, S:T], QB1[:, h, :])[n // 2][:, n % 2 * P:(n % 2 + 1) * P]
                return q, [(k[:, 0:512], 0), (k[:, 512:T], 512)], [V1[:, t, h * P:(h + 1) * P] for t in range(6)]
            blk = h // 2
            q = Q2[:, blk, n * P:(n + 1) * P] if h % 2 == 0 else X[:, 2 * blk + n // 2, S + n % 2 * P:S + (n % 2 + 1) * P]
            return (q, [(K2[:, blk, :], 0)],
                    [V2[:, t, P * blk:P * blk + P] for t in range(4)])

        V1 = VV

        def own_half(item):
            return 64 * (item[1] // 4) if item[0] in ("a", "b", "ca", "cb") else 64 * (item[1] % 2)

        def y_target(layer, pair):
            its = value_items(layer)
            kind, h, n = (its[pair] if layer == 1 else its[2 * pair])[:3]
            if layer == 0:
                blk = h // 2 + (4 if kind in ("b", "cb") else 0)
                if kind == "a":
                    return H[:, blk, n * P:(n + 1) * P]
                if kind == "b":
                    return H[:, blk, 0:S].rearrange("p (r c) -> p r c", c=GRID)[:, :, 16 * n:16 * n + 16]
                return H[:, blk, S + n * P:S + (n + 1) * P]
            if layer == 1:
                return H[:, h, n * P:(n + 1) * P]
            return H[:, 2 + h // 2, n * P:(n + 1) * P]

        def buffers(layer):
            return (PB, PT, YT) if layer < 2 else (PB2, PT2, YT2)

        def pair_index(blk, d, hx, j):
            return 14 * blk + 8 * d + (4 - d) * hx + j - d

        def s_slot(i):
            return psf[:, (i % 2) * 1024:(i % 2) * 1024 + 1024]

        PT_BANK = (4, 5)
        O_BANK, Y_BANK = 6, 7

        @block.tensor
        def _(pe):
            def attention(layer):
                its, vals = ATT[layer], value_items(layer)
                base, vbase, p2, ybase = att_base[layer], val_base[layer], pt2_base[layer], yt_base[layer]
                pb, pt, yt = buffers(layer)
                per = 2 if layer == 1 else 1
                seconds = [sum(key_tiles(v) > 4 for v in vals[:j + 1]) for j in range(len(vals))]

                def scores(i):
                    q, ks, _ = pieces(layer, its[i])
                    if i >= 2:
                        pe.wait_ge(probs_ready, base + i - 1)
                    for k, off_ in ks:
                        n = 1
                        for d in k.shape[1:]:
                            n *= d
                        mm = nc.tensor.matmul(s_slot(i)[:, off_:off_ + n], q, k, start=True, stop=True)
                    mm.then_inc(scores_ready, 1)

                def turn(j):
                    nt = key_tiles(vals[j])
                    if layer == 1:
                        pe.wait_ge(probs_mixed, j + 1)
                    else:
                        pe.wait_ge(probs_ready, base + j + 1)
                    if j >= 1:
                        pe.wait_ge(pt_copied_act, vbase + j)
                        if seconds[j - 1]:
                            pe.wait_ge(pt_copied_dve, p2 + seconds[j - 1])
                    for t in range(nt):
                        src = pb[:, 2 * (j % 2) if layer == 1 else j % 2, t * P:(t + 1) * P]
                        mm = nc.tensor.transpose(ps[:, PT_BANK[t // 4], (t % 4) * P:(t % 4 + 1) * P], src, ident[:, :])
                    mm.then_inc(pt_ready, 1)

                def values(j):
                    nt = key_tiles(vals[j])
                    vt = pieces(layer, vals[j] if layer != 1 else vals[j])[2]
                    pe.wait_ge(pt_copied_act, vbase + j + 1)
                    if nt > 4:
                        pe.wait_ge(pt_copied_dve, p2 + seconds[j])
                    if j >= 1:
                        pe.wait_ge(y_ready, vbase + j)
                    for t in range(nt):
                        mm = nc.tensor.matmul(ps[:, O_BANK, (j % 2) * P:(j % 2 + 1) * P], pt[:, j % 2, t * P:(t + 1) * P],
                                              vt[t], start=t == 0, stop=t == nt - 1)
                    mm.then_inc(o_ready, 1)

                def turn_y(y):
                    pe.wait_ge(y_ready, vbase + (y + 1) * (1 if layer == 1 else 2))
                    if y >= 1:
                        pe.wait_ge(yt_taken, ybase + y)
                    nc.tensor.transpose(ps[:, Y_BANK, (y % 2) * P:(y % 2 + 1) * P], yt[:, y % 2, :], ident[:, :]).then_inc(yt_ready, 1)

                nv = len(vals)
                ys = {(2 * y + 1 if per == 1 else y): y for y in range(nv if per == 2 else nv // 2)}
                for j in range(nv + 3):
                    if j < nv:
                        for i in range(per * j, per * j + per):
                            scores(i)
                    if 1 <= j <= nv:
                        turn(j - 1)
                    if 2 <= j <= nv + 1:
                        values(j - 2)
                    if j >= 3 and j - 3 in ys:
                        turn_y(ys[j - 3])

            def norm(i, cols):
                n = norm_phases.index(i)
                for kt in range(KT):
                    pe.wait_ge(sq_ready, KT * n + kt + 1)
                    for lo, hi, _ in ranges(cols):
                        mm = nc.tensor.matmul(psf[:, lo:hi], ones[:], H[:, kt, lo:hi], start=kt == 0, stop=kt == KT - 1)
                mm.then_inc(stats_ready, 1)

            def conv(i):
                n = conv_phases.index(i)
                pe.wait_ge(conv_ready, 2 * n + 2)
                for b in range(2):
                    mm = nc.tensor.matmul(ps[:, 0, :], ones4[:], AC[:, b, :], start=b == 0, stop=b == 1)
                mm.then_inc(ln_mean, 1)
                pe.wait_ge(ln_step, n + 1)
                for b in range(2):
                    mm = nc.tensor.matmul(ps[:, 1, :], ones4[:], AQ[:, b, :], start=b == 0, stop=b == 1)
                mm.then_inc(ln_mean, 1)

            def scan(i):
                n = scan_phases.index(i)
                for b in range(3):
                    blk = 3 * n + b
                    for d in range(2):
                        pe.wait_ge(unit_ready, 2 * blk + d + 1)
                        for hx in range(2):
                            rows = slice(64 * hx, 64 * hx + 64)
                            for j in range(d, 4):
                                r = pair_index(blk, d, hx, j)
                                if r >= 2:
                                    pe.wait_ge(pair_taken, r - 1)
                                for t in (range(j, 4) if d == 0 else range(j)):
                                    lhs, rhs = KF[rows, d, j * P:(j + 1) * P], QF[rows, d, t * P:(t + 1) * P]
                                    if t == j:
                                        lhs, rhs = KS[rows, j * P:(j + 1) * P], QR[rows, b, t * P:(t + 1) * P]
                                    x = {(2, 0): 0, (3, 1): 1, (3, 0): 2, (1, 3): 4, (0, 2): 3, (0, 3): 5}.get((t, j))
                                    if x is not None:
                                        rhs = QX[rows, x, :]
                                    mm = nc.tensor.matmul(ps[:, r % 2, t * P:(t + 1) * P], lhs, rhs, start=True, stop=True)
                                mm.then_inc(pair_ready, 1)
                        for li in range(7):
                            v = 14 * blk + 7 * d + li
                            pe.wait_ge(query_ready, v + 1)
                            if v >= 2:
                                pe.wait_ge(level_taken, v - 1)
                            for t in range(4):
                                mm = nc.tensor.matmul(ps[:, 2 + v % 2, t * P:(t + 1) * P], WL[:, 7 * d + li, t * P:(t + 1) * P],
                                                      level_queries(v)[:, t // 2, t % 2 * P:(t % 2 + 1) * P], start=True, stop=True)
                            mm.then_inc(level_ready, 1)
                        if d == 0:
                            if b >= 1:
                                turn_rec(blk - 1)
                            continue
                        pe.wait_ge(level_taken, 14 * blk + 14)
                        pe.wait_ge(pair_taken, pair_index(blk, 1, 1, 3) + 1)
                        for hx in range(2):
                            hh = 2 * blk + hx
                            if hh >= 2:
                                pe.wait_ge(so_taken, hh - 1)
                            for t in range(4):
                                for j in range(4):
                                    mm = nc.tensor.matmul(ps[:, SO_BANK[hx], t * P:(t + 1) * P], AM[:, hx, j, t * P:(t + 1) * P],
                                                          VR[:, j, P * b:P * b + P], start=j == 0, stop=j == 3)
                            mm.then_inc(so_ready, 1)
                turn_rec(3 * n + 2)

            def turn_rec(blk):
                pe.wait_ge(sy_ready, 2 * blk + 2)
                if blk >= 1:
                    pe.wait_ge(syt_taken, blk)
                for t in range(4):
                    mm = nc.tensor.transpose(ps[:, 5, t * P:(t + 1) * P], SO[:, t, :], ident[:, :])
                mm.then_inc(syt_ready, 1)

            pe.wait_ge(consts_in, N_CONST)
            pe.wait_ge(setup_done, 1)
            for i, ph in enumerate(PHASES):
                kind, layer = ph["kind"], ph["layer"]
                if kind == "norm":
                    norm(i, ph["cols"])
                elif kind == "final":
                    norm(i, S)
                elif kind == "linear":
                    for g in ph["groups"]:
                        product(pe, g)
                elif kind == "attention":
                    attention(layer)
                elif kind == "conv":
                    conv(i)
                elif kind == "scan":
                    scan(i)
                end_phase(pe, i)


        @block.scalar
        def _(act):
            chain = Chain(act, act_chain)

            def take(g):
                slot = psf[:, g.slot * 1024:(g.slot + 1) * 1024]
                if g.form == "turn":
                    act.wait_ge(vb_turned, g.index + 1)
                else:
                    act.wait_ge(chunk_done, g.done)
                freed = group_freed[g.slot]
                role, j = g.role, g.index
                if role == "rope_q":
                    nc.scalar.activation(QT[:, j, 0:g.cols], slot[:, 0:g.cols], ACT.Copy, scale=0.125).then_inc(freed, 1)
                    act.drain().then_inc(rope_in, 1)
                elif role == "rope_k":
                    nc.scalar.activation(KTT[:, j, 0:T], slot[:, 0:T], ACT.Copy).then_inc(freed, 1)
                    act.drain().then_inc(rope_in, 1)
                elif role == "va":
                    nc.scalar.activation(V0[:, 0:6, :], slot[:, 0:768].rearrange("p (t v) -> p t v", t=6), ACT.Copy).then_inc(freed, 1)
                elif role == "vbt":
                    grid = slot[:, 0:S].rearrange("p (r c) -> p r c", c=GRID)
                    for m, c0 in enumerate((0, 8, 24, 32)):
                        nc.scalar.activation(VBT[:, m * 256:(m + 1) * 256].rearrange("p (r c) -> p r c", c=32), grid[:, :, c0:c0 + 32], ACT.Copy)
                    nc.scalar.activation(VBT[:, 1024:1280], slot[:, S:T], ACT.Copy).then_inc(freed, 1)
                    act.drain().then_inc(vbt_ready, 1)
                elif role == "vb":
                    n = 8 if j == 0 else 2
                    nc.scalar.activation(V0[:, 6 + 8 * j:6 + 8 * j + n, :], slot[:, 0:n * P].rearrange("p (t v) -> p t v", t=n), ACT.Copy).then_inc(freed, 1)
                elif role == "relu":
                    nc.scalar.activation(HID1[:, j, 0:g.cols], slot[:, 0:g.cols], ACT.Relu).then_inc(freed, 1)
                    act.drain().then_inc(relu_ready, 1)
                elif role == "gate_a":
                    nc.scalar.activation(SGA[:, j, :], slot[:, 0:S], ACT.Sigmoid).then_inc(freed, 1)
                    act.drain().then_inc(sig_ready, 1)
                elif role == "q2":
                    nc.scalar.activation(Q2[0:64, j, :], slot[0:64, 0:S], ACT.Copy, scale=0.125)
                    nc.scalar.activation(X[64:P, 2 * j:2 * j + 2, S:T], slot[64:P, 0:S].rearrange("p (a t) -> p a t", a=2), ACT.Copy,
                                         scale=0.125).then_inc(freed, 1)
                elif role == "v2":
                    nc.scalar.activation(V2[:, :, j * P:(j + 1) * P], slot[:, 0:S].rearrange("p (t v) -> p t v", t=4), ACT.Copy).then_inc(freed, 1)
                elif role in ("silu_q", "silu_g"):
                    dst = QR if role == "silu_q" else GR
                    nc.scalar.activation(dst[:, j, :], slot[:, 0:S], ACT.Silu).then_inc(freed, 1)
                elif role == "z":
                    nc.scalar.activation(LF[:, j, :], slot[:, 0:S], ACT.Sigmoid)
                    nc.scalar.activation(KR[:, j, :], slot[:, 0:S], ACT.Sigmoid, scale=-1.0).then_inc(freed, 1)
                    act.drain().then_inc(z_ready, 1)
                elif role.startswith("ffn"):
                    n = ffn_groups.index(g)
                    blk = j if role == "ffn_gate" else NB2 + j
                    u = (UG if role == "ffn_gate" else UV)[:, j % 2, :]
                    if n >= 4:
                        act.wait_ge(hid_ready, n // 2 - 1)
                    nc.scalar.activation(u, slot[:, 0:S], ACT.Copy, scale=CFW[:, blk, 1:2]).then_inc(conv_first, 1)
                    if role == "ffn_val" and j >= 1:
                        gelu(n // 2 - 1)
                    if role == "ffn_val" and j == NB2 - 1:
                        gelu(n // 2)

            def gelu(n):
                act.wait_ge(conv_out, 2 * n + 1)
                if n >= 2:
                    act.wait_ge(hid_ready, n - 1)
                nc.scalar.activation(GL[:, n % 2, :], UG[:, n % 2, :], ACT.Gelu).then_inc(gelu_ready, 1)

            def attention(layer):
                its, vals = ATT[layer], value_items(layer)
                base, vbase, ybase = att_base[layer], val_base[layer], yt_base[layer]
                pb, pt, yt = buffers(layer)
                per = 2 if layer == 1 else 1

                def probs(i):
                    item = its[i]
                    n = key_tiles(item) * P
                    act.wait_ge(max_ready, base + i + 1)
                    if layer != 1 and i >= 2:
                        act.wait_ge(pt_ready, vbase + i - 1)
                    if layer == 1 and i >= 4:
                        act.wait_ge(pt_ready, vbase + i // 2 - 1)
                    if item[0] in ("a", "ca"):
                        nc.scalar.activation(small[:, 8 + i % 4:9 + i % 4], SINK[:, item[1]:item[1] + 1], ACT.Exp,
                                             bias=small[:, i % 4:i % 4 + 1])
                    nc.scalar.activation(pb[:, i % 4 if layer == 1 else i % 2, 0:n], s_slot(i)[:, 0:n], ACT.Exp, bias=small[:, i % 4:i % 4 + 1],
                                         accum_out=small[:, 4 + i % 4:5 + i % 4]).then_inc(probs_ready, 1)

                def copy_pt(j):
                    n = min(key_tiles(vals[j]), 4) * P
                    act.wait_ge(pt_ready, vbase + j + 1)
                    if j >= 2:
                        act.wait_ge(o_ready, vbase + j - 1)
                    nc.scalar.activation(pt[:, j % 2, 0:n], ps[:, PT_BANK[0], 0:n], ACT.Copy).then_inc(pt_copied_act, 1)

                def take_o(j):
                    act.wait_ge(o_ready, vbase + j + 1)
                    pair = j if layer == 1 else j // 2
                    if layer == 1:
                        if pair >= 2:
                            act.wait_ge(yt_ready, ybase + pair - 1)
                        o = ps[:, O_BANK, (j % 2) * P:(j % 2 + 1) * P]
                        act.wait_ge(root_scale, j + 1)
                        nc.scalar.activation(SUBT, o, ACT.Square, scale=small[:, 28 + j % 4:29 + j % 4],
                                             accum_out=small[:, 20 + j % 2:21 + j % 2]).then_inc(o_squares, 1)
                        act.wait_ge(o_inv, j + 1)
                        nc.scalar.activation(yt[:, j % 2, :], o, ACT.Copy, scale=small[:, 24 + j % 2:25 + j % 2]).then_inc(y_ready, 1)
                        return
                    act.wait_ge(inv_ready, base + j + 1)
                    if j % 2 == 0 and pair >= 2:
                        act.wait_ge(yt_ready, ybase + pair - 1)
                    nc.scalar.activation(yt[:, pair % 2, 64 * (j % 2):64 * (j % 2) + 64], ps[:, O_BANK, (j % 2) * P + own_half(vals[j]):(j % 2) * P + own_half(vals[j]) + 64],
                                         ACT.Copy, scale=small[:, 12 + j % 4:13 + j % 4]).then_inc(y_ready, 1)

                nv = len(vals)
                for j in range(nv + 2):
                    if j < nv:
                        for i in range(per * j, per * j + per):
                            probs(i)
                    if 1 <= j <= nv:
                        copy_pt(j - 1)
                    if j >= 2:
                        take_o(j - 2)

            def norm(i, ph, final):
                n = norm_phases.index(i)
                cols = S if final else ph["cols"]
                layer = ph["layer"]
                for kt in range(KT):
                    nc.scalar.activation(H[:, kt, 0:cols], X[:, kt, 0:cols], ACT.Square).then_inc(sq_ready, 1)
                act.wait_ge(stats_ready, n + 1)
                nc.scalar.activation(R[:, 0:cols], psf[:, 0:cols], ACT.Sqrt, bias=small[:, 40:41]).then_inc(rstd_ready, 1)
                if final:
                    return
                for kt in range(KT):
                    for lo, hi, s in ranges(cols):
                        act.wait_ge(scaled_ready, scaled_before[i] + kt + 1)
                        nc.scalar.activation(H[:, kt, lo:hi], H[:, kt, lo:hi], ACT.Identity,
                                             scale=gs[:, layer, ph["which"] - 1, kt, s:s + 1],
                                             bias=mod[:, layer, (SH1 if ph["which"] == 1 else SH2) + kt, s:s + 1])

            def conv(i):
                n = conv_phases.index(i)
                for b in range(2):
                    act.wait_ge(ln_x, 3 * n + 1)
                    nc.scalar.activation(AQ[:, b, :], AC[:, b, :], ACT.Square)
                act.drain().then_inc(ln_step, 1)
                act.wait_ge(ln_mean, 2 * n + 2)
                nc.scalar.activation(R[:, 0:S], ps[:, 1, :], ACT.Sqrt, bias=small[:, 40:41]).then_inc(rstd_ready, 1)
                for b in range(2):
                    act.wait_ge(ln_x, 3 * n + 2 + b)
                    nc.scalar.activation(H[:, b, 0:S], AC[:, b, :], ACT.Silu, scale=CAV[:, b, 1:2], bias=CAV[:, b, 2:3])

            def fetch_mod(k):
                layer, nb, _ = mod_items[k]
                if k >= ARING:
                    act.wait_ge(ada_used, k - ARING + 1)
                act.dma_start(aring[:, k % ARING, :], a[f"ada{layer}"][nb]).then_inc(ada_arrived[k % ARING], 16)

            def fetch_mods(share):
                for k in share:
                    if k + ARING < len(mod_items):
                        fetch_mod(k + ARING)

            def logarithms(n):
                for b in range(6):
                    act.wait_ge(gate_clamped, 6 * n + b + 1)
                    nc.scalar.activation(LF[:, b, :], LF[:, b, :], ACT.Ln)
                    nc.scalar.activation(LTMP[:, b, :], LTMP[:, b, :], ACT.Ln).then_inc(log_ready, 1)

            def scan(i):
                n = scan_phases.index(i)

                def decays(u):
                    if u >= 6:
                        return
                    d = u % 2
                    act.wait_ge(diff_ready, 6 * n + u + 1)
                    nc.scalar.activation(WL[:, 7 * d:7 * d + 7, :], WL[:, 7 * d:7 * d + 7, :], ACT.Exp)
                    nc.scalar.activation(QF[:, d, :], QF[:, d, :], ACT.Exp)
                    nc.scalar.activation(KF[:, d, :], KF[:, d, :], ACT.Exp)
                    nc.scalar.activation(ET[:, 3 * d:3 * d + 3], ET[:, 3 * d:3 * d + 3], ACT.Exp).then_inc(decay_ready, 1)

                decays(0)
                for u in range(6):
                    blk, d = 3 * n + u // 2, u % 2
                    decays(u + 1)
                    for hx in range(2):
                        hh = 2 * blk + hx
                        for j in range(d, 4):
                            r = pair_index(blk, d, hx, j)
                            act.wait_ge(pair_ready, r + 1)
                            if j == 0 and hh >= 2:
                                act.wait_ge(so_ready, hh - 1)
                            lo, hi = (j * P, S) if d == 0 else (0, j * P)
                            nc.scalar.activation(AM[:, hx, j, lo:hi], ps[:, r % 2, lo:hi], ACT.Copy).then_inc(pair_taken, 1)
                    if d == 0:
                        continue
                    for hx in range(2):
                        hh = 2 * blk + hx
                        act.wait_ge(so_ready, hh + 1)
                        if hh >= 2:
                            act.wait_ge(sor_ready, hh - 1)
                        nc.scalar.activation(SQR[:, hx, :].rearrange("p (t v) -> p t v", t=4), own_values(hx), ACT.Square, scale=0.125).then_inc(sosq_ready, 1)

            act.wait_ge(consts_in, N_CONST)
            nc.scalar.activation(X_SG, csil[:], ACT.Sigmoid).then_inc(sig_ready, 1)
            for k in range(ARING):
                fetch_mod(k)
            act.wait_ge(setup_done, 1)
            for i, ph in enumerate(PHASES):
                kind, layer = ph["kind"], ph["layer"]
                if i in first_loads:
                    act.wait_ge(layer_in, loads_until(i))
                if i == first1:
                    act.wait_ge(lam_sums, 1)
                    nc.scalar.activation(LAMS[:, 2:4], LAMS[:, 0:2], ACT.Exp).then_inc(lam_exp, 1)
                if i in first23:
                    act.wait_ge(gam_ready, first23.index(i) + 1)
                    nc.scalar.activation(GTMP[:, 1:3], GTMP[:, 1:3], ACT.Exp).then_inc(gam_exp, 1)
                if i == cond2_phase:
                    act.wait_ge(cond2_in, 16)
                    nc.scalar.activation(ARENA[:, 15500:15500 + D], csil[:, 0, :], ACT.Sigmoid).then_inc(cond2_sig, 1)
                if kind == "ada":
                    fetch_mods(mod_share(i))
                elif kind == "norm":
                    norm(i, ph, False)
                elif kind == "final":
                    norm(i, ph, True)
                elif kind == "linear":
                    for n, g in enumerate(ph["groups"]):
                        if g.by in ("act", "act+dve"):
                            take(g)
                        fetch_mods(mod_share(i, n, len(ph["groups"])))
                    if i in mixer_phases:
                        logarithms(mixer_phases.index(i))
                elif kind == "attention":
                    attention(layer)
                elif kind == "conv":
                    conv(i)
                elif kind == "scan":
                    scan(i)
                end_phase(act, i)

        @block.vector
        def _(dve):
            chain = Chain(dve, dve_chain)

            def part_keys(j):
                nc.vector.memset(KP1[0:64, j, :], 0.0)
                chain(nc.vector.tensor_copy(KP1[64:P, j, :], KTT[64:P, j, :]))
                nc.vector.memset(KTT[64:P, j, :], 0.0)

            def take(g):
                slot = psf[:, g.slot * 1024:(g.slot + 1) * 1024]
                freed = group_freed[g.slot]
                role, j = g.role, g.index
                if role in ("rope_q", "rope_k"):
                    n = rope_groups.index(g)
                    buf = (QT if role == "rope_q" else KTT)[:, j, 0:S]
                    dve.wait_ge(rope_in, n + 1)
                    nc.vector.stream_shuffle(ROTB[:, n % 2, 0:S], buf, ROT).then_inc(rot_ready, 1)
                    dve.wait_ge(rot_ready, n + 1)
                    chain(nc.vector.tensor_tensor(buf, buf, COS, ALU.mult))
                    dve.wait_ge(rot_scaled, n + 1)
                    chain(nc.vector.tensor_tensor(buf, buf, ROTB[:, n % 2, 0:S], ALU.add))
                    if g.weight == "even_in" and role == "rope_k":
                        part_keys(j)
                    if g.weight == "odd_in" and role == "rope_q":
                        nc.vector.tensor_copy(QT[64:P, j, S:T], QT[64:P, j, 0:2 * P])
                        chain(nc.vector.tensor_copy(QB1[64:P, j, :], QT[64:P, j, 2 * P:S]))
                        nc.vector.memset(QT[64:P, j, 0:S], 0.0)
                        nc.vector.memset(QT[0:64, j, S:T], 0.0)
                        nc.vector.memset(QB1[0:64, j, :], 0.0)
                    return
                if role.startswith("ffn"):
                    n = ffn_groups.index(g)
                    blk = j if role == "ffn_gate" else NB2 + j
                    u = (UG if role == "ffn_gate" else UV)[:, j % 2, :]
                    dve.wait_ge(conv_first, n + 1)
                    chain(nc.vector.scalar_tensor_tensor(out=u[:, 1:S], in0=slot[:, 0:S - 1], scalar=CFW[:, blk, 0:1],
                                                         in1=u[:, 1:S], op0=ALU.mult, op1=ALU.add))
                    nc.vector.scalar_tensor_tensor(out=u[:, 0:S - 1], in0=slot[:, 1:S], scalar=CFW[:, blk, 2:3],
                                                   in1=u[:, 0:S - 1], op0=ALU.mult, op1=ALU.add).then_inc(freed, 1)
                    dve.drain().then_inc(conv_out, 1)
                    return
                dve.wait_ge(chunk_done, g.done)
                if role == "plain_q":
                    for m in range(4):
                        nc.vector.tensor_scalar(QT[:, j, m * P:(m + 1) * P].rearrange("p (r c) -> p r c", c=16),
                                                slot[:, 0:S].rearrange("p (r c) -> p r c", c=GRID)[:, :, 16 * m:16 * m + 16],
                                                0.125, None, ALU.mult)
                    nc.vector.tensor_scalar(QT[:, j, S:T], slot[:, S:T], 0.125, None, ALU.mult).then_inc(freed, 1)
                elif role == "plain_k":
                    nc.vector.tensor_copy(KTT[:, j, 0:T], slot[:, 0:T]).then_inc(freed, 1)
                    dve.wait_ge(freed, g.n // NSLOT + 1)
                    part_keys(j)
                elif role == "v1":
                    nc.vector.tensor_copy(V1[:, :, j * P:(j + 1) * P], slot[:, 0:768].rearrange("p (t v) -> p t v", t=6)).then_inc(freed, 1)
                elif role == "k2":
                    nc.vector.tensor_copy(K2[:, j, :], slot[:, 0:S]).then_inc(freed, 1)
                elif role == "vr":
                    nc.vector.tensor_copy(VR[:, :, j * P:(j + 1) * P], slot[:, 0:S].rearrange("p (t v) -> p t v", t=4)).then_inc(freed, 1)
                elif role == "val_a":
                    n = gate_groups.index([x for x in gate_groups if x.weight == g.weight and x.index == j][0])
                    dve.wait_ge(sig_ready, n + 2)
                    nc.vector.tensor_tensor(AP_[:, j, PAD:PAD + S], slot[:, 0:S], SGA[:, j, :], ALU.mult).then_inc(freed, 1)
                elif role == "residual":
                    rs = ranges(g.cols)
                    layer = int(g.weight[-1])
                    for lo, hi, s in rs:
                        x = nc.vector.scalar_tensor_tensor(out=X[:, j, lo:hi], in0=slot[:, lo:hi], scalar=mod[:, layer, g.extra + j, s:s + 1],
                                                           in1=X[:, j, lo:hi], op0=ALU.mult, op1=ALU.add)
                    x.then_inc(freed, 1)

            def attention(layer):
                its, vals = ATT[layer], value_items(layer)
                base, vbase, ybase = att_base[layer], val_base[layer], yt_base[layer]
                pb, pt, yt = buffers(layer)
                per = 2 if layer == 1 else 1

                def maxima(i):
                    item = its[i]
                    n = key_tiles(item) * P
                    dve.wait_ge(scores_ready, base + i + 1)
                    s = s_slot(i)
                    if item[0] == "a":
                        q = item[2]
                        masks = []
                        if q > 0:
                            masks.append((C, 0))
                        if q < 3:
                            masks.append((C + P if q == 0 else 512, 1))
                        for off_, m in masks:
                            chain(nc.vector.tensor_tensor(s[:, off_:off_ + P], s[:, off_:off_ + P], WIN[:, m, :], ALU.add))
                    if item[0] == "b":
                        v = (0, 1, 1, 2)[item[2]]
                        chain(nc.vector.tensor_tensor(s[:, 0:256], s[:, 0:256], BM[:, item[1], v, :], ALU.add))
                    if item[0] == "e":
                        o = 384 - P * item[2]
                        chain(nc.vector.tensor_tensor(s[:, 0:512], s[:, 0:512], BIAS[:, item[1], o:o + 512], ALU.add))
                    nm = small[:, i % 4:i % 4 + 1]
                    if item[0] in ("a", "ca"):
                        chain(nc.vector.tensor_reduce(small[:, 48 + i % 8:49 + i % 8], s[:, 0:n], AX_X, ALU.max))
                        nc.vector.tensor_scalar(nm, small[:, 48 + i % 8:49 + i % 8], SINK[:, item[1]:item[1] + 1], -1.0, ALU.max, ALU.mult).then_inc(max_ready, 1)
                    else:
                        nc.vector.tensor_reduce(nm, s[:, 0:n], AX_X, ALU.max, negate=True).then_inc(max_ready, 1)

                def inverse(i):
                    item = its[i]
                    dve.wait_ge(probs_ready, base + i + 1)
                    l = small[:, 4 + i % 4:5 + i % 4]
                    inv = small[:, 12 + i % 4:13 + i % 4]
                    if item[0] in ("a", "ca"):
                        chain(nc.vector.tensor_tensor(l, l, small[:, 8 + i % 4:9 + i % 4], ALU.add))
                    if layer == 1 and i % 2:
                        chain(nc.vector.reciprocal(inv, l))
                        i0 = i - 1
                        nc.vector.scalar_tensor_tensor(out=inv, in0=inv, scalar=LAMS[:, 7:8], in1=small[:, 4 + i0 % 4:5 + i0 % 4],
                                                       op0=ALU.mult, op1=ALU.mult).then_inc(inv_ready, 1)
                    else:
                        nc.vector.reciprocal(inv, l).then_inc(inv_ready, 1)

                def mix(j):
                    dve.wait_ge(inv_ready, base + 2 * j + 2)
                    n = 6 * P
                    i1 = 2 * j + 1
                    nc.vector.scalar_tensor_tensor(out=pb[:, 2 * (j % 2), 0:n], in0=pb[:, 2 * (j % 2) + 1, 0:n],
                                                   scalar=small[:, 12 + i1 % 4:13 + i1 % 4], in1=pb[:, 2 * (j % 2), 0:n],
                                                   op0=ALU.mult, op1=ALU.add).then_inc(probs_mixed, 1)
                    i0 = 2 * j
                    nc.vector.tensor_scalar(small[:, 28 + j % 4:29 + j % 4], small[:, 12 + i0 % 4:13 + i0 % 4], P ** -0.5, None,
                                            ALU.mult).then_inc(root_scale, 1)

                def copy_pt(j):
                    n = key_tiles(vals[j])
                    if n <= 4:
                        return
                    dve.wait_ge(pt_ready, vbase + j + 1)
                    if j >= 2:
                        dve.wait_ge(o_ready, vbase + j - 1)
                    nc.vector.tensor_copy(pt[:, j % 2, 512:n * P], ps[:, PT_BANK[1], 0:(n - 4) * P]).then_inc(pt_copied_dve, 1)

                def take_y(y):
                    dve.wait_ge(yt_ready, ybase + y + 1)
                    src = ps[:, Y_BANK, (y % 2) * P:(y % 2 + 1) * P]
                    dst = y_target(layer, y)
                    if layer == 1:
                        nc.vector.tensor_scalar(dst, src, SUBG, 1.0 - LAM_INIT, ALU.mult, ALU.mult).then_inc(yt_taken, 1)
                    else:
                        if len(dst.shape) == 3:
                            src = src.rearrange("p (r c) -> p r c", c=16)
                        nc.vector.tensor_copy(dst, src).then_inc(yt_taken, 1)

                nv = len(vals)
                ys = {(2 * y + 1 if per == 1 else y): y for y in range(nv if per == 2 else nv // 2)}
                for j in range(nv + 3):
                    if j < nv:
                        for i in range(per * j, per * j + per):
                            maxima(i)
                    if layer == 1 and 1 <= j <= nv:
                        inverse(2 * j - 2)
                        inverse(2 * j - 1)
                        mix(j - 1)
                    elif 1 <= j <= nv:
                        inverse(j - 1)
                    if 1 <= j <= nv:
                        copy_pt(j - 1)
                    if j >= 3 and j - 3 in ys:
                        take_y(ys[j - 3])

            def modulate(share):
                for k in share:
                    layer, nb, w = mod_items[k]
                    dve.wait_ge(ada_arrived[k % ARING], 16 * (k // ARING + 1))
                    for c in reversed(range(w)):
                        wt = aring[:, k % ARING, :]
                        if c == 1:
                            x = nc.vector.tensor_tensor_reduce(JUNK[:], wt, csil[:, 1, :], 1.0, adab[:, layer, nb:nb + 1],
                                                               ALU.mult, ALU.add, mod[:, layer, nb, 1:2])
                            x.then_inc(ada_first, 1)
                            firsts[0] += 1
                            dve.wait_ge(ada_first, firsts[0])
                        else:
                            nc.vector.tensor_tensor_reduce(wt, wt, csil[:, 0, :], 1.0, adab[:, layer, nb:nb + 1],
                                                           ALU.mult, ALU.add, mod[:, layer, nb, 0:1]).then_inc(ada_used, 1)

            firsts = [0]

            def norm(i, ph, final):
                n = rstd_order.index(i)
                cols = S if final else ph["cols"]
                if not final:
                    layer, which = ph["layer"], ph["which"] - 1
                    o = (SC1, SC2)[which]
                    dve.wait_ge(ada_used, mod_base[i])
                    for s_ in range(2 if cols == T else 1):
                        chain(nc.vector.scalar_tensor_tensor(out=gs[:, layer, which, :, s_], in0=mod[:, layer, o:o + KT, s_], scalar=1.0,
                                                             in1=gvec[:, layer, which, :], op0=ALU.add, op1=ALU.mult))
                dve.wait_ge(rstd_ready, n + 1)
                chain(nc.vector.reciprocal(R[:, 0:cols], R[:, 0:cols]))
                for kt in range(KT):
                    if not final:
                        nc.vector.tensor_tensor(H[:, kt, 0:cols], X[:, kt, 0:cols], R[:, 0:cols], ALU.mult).then_inc(scaled_ready, 1)
                    elif ph["layer"] == 0:
                        nc.vector.scalar_tensor_tensor(out=X[:, kt, 0:S], in0=X[:, kt, 0:S], scalar=fin_g[:, 0, kt:kt + 1],
                                                       in1=R[:, 0:S], op0=ALU.mult, op1=ALU.mult)
                    else:
                        nc.vector.scalar_tensor_tensor(out=H[:, kt, 0:S], in0=X[:, kt, 0:S], scalar=fin_g[:, 1, kt:kt + 1],
                                                       in1=R[:, 0:S], op0=ALU.mult, op1=ALU.mult).then_inc(out_ready, 1)

            def bias0():
                for v, shift in enumerate((0, -8, -16)):
                    for h in range(8):
                        src = RPBW[:, h, 248 - shift:249 - shift]
                        src = bass.AP(src.tensor, src.offset, [src.ap[0], [-31, 8], [-1, 32]])
                        nc.vector.tensor_tensor(BM[:, h, v, :].rearrange("p (r c) -> p r c", r=8), src,
                                                NA[:, v, :].rearrange("p (r c) -> p r c", r=8), ALU.add)

            def lam1():
                for m in range(2):
                    chain(nc.vector.tensor_tensor(LAMV[:, 2 * m, :], LAMV[:, 2 * m, :], LAMV[:, 2 * m + 1, :], ALU.mult))
                    chain(nc.vector.reduce_sum(LAMS[:, m:m + 1], LAMV[:, 2 * m, :], AX_X))
                dve.drain().then_inc(lam_sums, 1)
                dve.wait_ge(lam_exp, 1)
                chain(nc.vector.tensor_tensor(LAMS[:, 4:5], LAMS[:, 3:4], LAMS[:, 2:3], ALU.subtract))
                chain(nc.vector.tensor_scalar(LAMS[:, 7:8], LAMS[:, 4:5], -LAM_INIT, None, ALU.add))

            def bounds(k):
                g0, g1 = GAM[:, 0].rearrange("p l b -> p (l b)"), GAM[:, 1].rearrange("p l b -> p (l b)")
                chain(nc.vector.tensor_tensor(GTMP[:, 0], g0, g1, ALU.max))
                chain(nc.vector.tensor_tensor(GTMP[:, 1], g0, GTMP[:, 0], ALU.subtract))
                chain(nc.vector.tensor_tensor(GTMP[:, 2], g1, GTMP[:, 0], ALU.subtract))
                dve.drain().then_inc(gam_ready, 1)
                dve.wait_ge(gam_exp, k + 1)
                chain(nc.vector.tensor_tensor(GTMP[:, 0], GTMP[:, 1], GTMP[:, 2], ALU.add))
                chain(nc.vector.reciprocal(GTMP[:, 0], GTMP[:, 0]))
                chain(nc.vector.tensor_tensor(GTMP[:, 1], GTMP[:, 1], GTMP[:, 0], ALU.mult))
                chain(nc.vector.tensor_tensor(GTMP[:, 2], GTMP[:, 2], GTMP[:, 0], ALU.mult))
                if k == 0:
                    chain(nc.vector.tensor_tensor(LB, GTMP[:, 1], GTMP[:, 1], ALU.subtract))
                else:
                    chain(nc.vector.tensor_tensor(GTMP[:, 2], GTMP[:, 1], GTMP[:, 2], ALU.add))
                    chain(nc.vector.tensor_tensor(LB, GTMP[:, 2], GTMP[:, 1], ALU.subtract))
                chain(nc.vector.tensor_scalar(OMLB, LB, -1.0, 1.0, ALU.mult, ALU.add))

            def taps(ts):
                for t in ts:
                    for b in range(2):
                        if t == 0:
                            x = nc.vector.tensor_scalar(AC[:, b, :], AP_[:, b, 0:S], CAW[:, b, 0:1], CAV[:, b, 0:1], ALU.mult, ALU.add)
                        else:
                            x = nc.vector.scalar_tensor_tensor(out=AC[:, b, :], in0=AP_[:, b, t:t + S], scalar=CAW[:, b, t:t + 1],
                                                               in1=AC[:, b, :], op0=ALU.mult, op1=ALU.add)
                        if t == CONV - 1:
                            x.then_inc(conv_ready, 1)
                        elif b == 1:
                            chain(x)

            def clamps(n, b):
                dve.wait_ge(z_ready, 6 * n + b + 1)
                chain(nc.vector.tensor_scalar(LF[:, b, :], LF[:, b, :], OMLB[:, b:b + 1], LB[:, b:b + 1], ALU.mult, ALU.add))
                chain(nc.vector.tensor_scalar(LF[:, b, :], LF[:, b, :], TINY, None, ALU.max))
                nc.vector.tensor_scalar(KR[:, b, :], KR[:, b, :], OMLB[:, b:b + 1], None, ALU.mult)
                chain(nc.vector.tensor_scalar(LTMP[:, b, :], LF[:, b, :], SPLIT, 1.0, ALU.mult, ALU.min))
                chain(nc.vector.tensor_scalar(LF[:, b, :], LF[:, b, :], 1.0 / SPLIT, None, ALU.max))
                dve.drain().then_inc(gate_clamped, 1)

            def conv(i):
                n = conv_phases.index(i)
                dve.wait_ge(ln_mean, 2 * n + 1)
                dve.wait_ge(conv_ready, 2 * n + 2)
                for b in range(2):
                    x = nc.vector.tensor_tensor(AC[:, b, :], AC[:, b, :], ps[:, 0, :], ALU.subtract)
                x.then_inc(ln_x, 1)
                dve.wait_ge(ln_x, 3 * n + 1)
                dve.wait_ge(rstd_ready, rstd_order.index(i) + 1)
                chain(nc.vector.reciprocal(R[:, 0:S], R[:, 0:S]))
                for b in range(2):
                    nc.vector.tensor_tensor(AC[:, b, :], AC[:, b, :], R[:, 0:S], ALU.mult).then_inc(ln_x, 1)

            def bias2():
                for h in (5, 4, 3, 2):
                    nc.vector.scalar_tensor_tensor(out=BIAS[:, h, :], in0=BIAS[:, 0, :], scalar=-SLOPES[h], in1=BIAS[:, 1, :],
                                                   op0=ALU.mult, op1=ALU.add)
                chain(nc.vector.tensor_copy(PB2[:, 0:2, :].rearrange("p s t -> p (s t)")[:, 0:896], BIAS[:, 0, :]))
                chain(nc.vector.scalar_tensor_tensor(out=BIAS[:, 0, :], in0=BIAS[:, 0, :], scalar=-SLOPES[0], in1=BIAS[:, 1, :],
                                                     op0=ALU.mult, op1=ALU.add))
                chain(nc.vector.scalar_tensor_tensor(out=BIAS[:, 1, :], in0=PB2[:, 0:2, :].rearrange("p s t -> p (s t)")[:, 0:896],
                                                     scalar=-SLOPES[1], in1=BIAS[:, 1, :], op0=ALU.mult, op1=ALU.add))

            def scan(i):
                n = scan_phases.index(i)
                chain(nc.vector.memset(E[:, :, :, 0:1], 0.0))
                for b in range(6):
                    for t in range(4):
                        nc.vector.tensor_tensor_scan(E[:, b, t, 1:129], ONE1, LF[:, b, t * P:(t + 1) * P], 0.0, ALU.mult, ALU.add)
                dve.drain().then_inc(dve_chain, 1)
                chain.n += 1
                dve.wait_ge(dve_chain, chain.n)

                def exponents(u):
                    if u >= 6:
                        return
                    b, d = u // 2, u % 2
                    e = E[:, 3 * d + b]
                    src = e[:, :, 1 - d:129 - d]
                    for li, m in enumerate(LEVELS):
                        nb = 64 // m
                        w = WL[:, 7 * d + li, :].rearrange("p (t b x m) -> p t x b m", t=4, x=2, m=m)
                        x = src.rearrange("p t (b x m) -> p t x b m", x=2, m=m)
                        bd = (e[:, :, m:129:2 * m] if m < 64 else e[:, :, 64:65])[:, :, 0:nb].unsqueeze(3).broadcast_to([P, 4, nb, m])
                        nc.vector.tensor_tensor(w[:, :, 0], bd, x[:, :, 0], ALU.subtract)
                        nc.vector.tensor_tensor(w[:, :, 1], x[:, :, 1], bd, ALU.subtract)
                    qf = QF[:, d].rearrange("p (t k) -> p t k", t=4)
                    kf = KF[:, d].rearrange("p (t k) -> p t k", t=4)
                    ends = e[:, :, 128:129].broadcast_to([P, 4, P])
                    nc.vector.tensor_copy((qf, kf)[d], src)
                    nc.vector.tensor_tensor((kf, qf)[d], ends, src, ALU.subtract)
                    nc.vector.tensor_copy(ET[:, 3 * d:3 * d + 2], e[:, 1:3, 128])
                    if d == 0:
                        nc.vector.tensor_tensor(KS[:], KR[:, b, :], KR[:, 3 + b, :], ALU.add)
                    nc.vector.tensor_tensor(ET[:, 3 * d + 2:3 * d + 3], e[:, 1, 128:129], e[:, 2, 128:129], ALU.add)
                    dve.drain().then_inc(diff_ready, 1)

                def weigh(u):
                    if u >= 6:
                        return
                    b, d = u // 2, u % 2
                    dve.wait_ge(decay_ready, 6 * n + u + 1)
                    nc.vector.tensor_tensor(KF[:, d, :], KF[:, d, :], KR[:, 3 * d + b, :], ALU.mult)
                    chain(nc.vector.tensor_tensor(QF[:, d, :], QF[:, d, :], QR[:, b, :], ALU.mult))
                    for x in range(3):
                        t = (2, 3, 3)[x] if d == 0 else (0, 1, 0)[x]
                        nc.vector.tensor_scalar(QX[:, 3 * d + x, :], QF[:, d, t * P:(t + 1) * P], ET[:, 3 * d + x:3 * d + x + 1], None, ALU.mult)
                    for li, m in enumerate(LEVELS):
                        w = WL[:, 7 * d + li, :].rearrange("p (g x m) -> p x g m", x=2, m=m)[:, d]
                        k = KR[:, 3 * d + b, :].rearrange("p (g x m) -> p x g m", x=2, m=m)[:, d]
                        x = nc.vector.tensor_tensor(w, w, k, ALU.mult)
                    x.then_inc(unit_ready, 1)

                def merge(blk, d):
                    dve.wait_ge(pair_taken, pair_index(blk, d, 1, 3) + 1)
                    for li, m in enumerate(LEVELS):
                        v = 14 * blk + 7 * d + li
                        dve.wait_ge(level_ready, v + 1)
                        if v >= 1:
                            dve.wait_ge(level_taken, v)
                        nb = 64 // m
                        mask = LEVM.bitcast(I32)[:, d, li, :].rearrange("p (b m) -> p b m", m=m).unsqueeze(1).broadcast_to([P, 4, nb, m])
                        for hx in range(2):
                            dst = diagonal(hx).rearrange("p t (b x m) -> p t x b m", x=2, m=m)[:, :, 1 - d]
                            src = ps[:, 2 + v % 2, :].rearrange("p (t h b m) -> p h t b m", t=4, h=2, m=m)[:, hx]
                            x = nc.vector.copy_predicated(dst, mask, src)
                        x.then_inc(level_taken, 1)

                def sums(blk, hx):
                    hh = 2 * blk + hx
                    dve.wait_ge(sosq_ready, hh + 1)
                    if hh >= 2:
                        dve.wait_ge(so_inv, hh - 1)
                    nc.vector.reduce_sum(small[:, 24 + 4 * hx:28 + 4 * hx], SQR[:, hx, :].rearrange("p (t v) -> p t v", t=4), AX_X).then_inc(sor_ready, 1)

                def output(blk, hx):
                    hh = 2 * blk + hx
                    dve.wait_ge(so_inv, hh + 1)
                    if hx == 0 and blk >= 1:
                        dve.wait_ge(syt_ready, blk)
                    for t in range(4):
                        x = nc.vector.tensor_scalar(SO[:, t, 64 * hx:64 * hx + 64], own_values(hx)[:, t],
                                                    small[:, 36 + 16 * hx + t:37 + 16 * hx + t], None, ALU.mult)
                    x.then_inc(so_taken, 1)
                    dve.drain().then_inc(sy_ready, 1)

                def finish(blk):
                    dve.wait_ge(syt_ready, blk + 1)
                    b = blk % 3
                    nc.vector.scalar_tensor_tensor(out=H[:, 5 + b, 0:S], in0=ps[:, 5, :], scalar=RNW[:, b:b + 1], in1=GR[:, b, :],
                                                   op0=ALU.mult, op1=ALU.mult).then_inc(syt_taken, 1)

                exponents(0)
                exponents(1)
                weigh(0)
                for u in range(6):
                    blk, d = 3 * n + u // 2, u % 2
                    if d == 0 and u:
                        output(blk - 1, 0)
                        output(blk - 1, 1)
                    merge(blk, d)
                    weigh(u + 1)
                    if d == 0 and u:
                        finish(blk - 1)
                    exponents(u + 2)
                    if d == 1:
                        sums(blk, 0)
                        sums(blk, 1)
                output(3 * n + 2, 0)
                output(3 * n + 2, 1)
                finish(3 * n + 2)

            nc.vector.memset(ones[:], 1.0 / D)
            nc.vector.memset(ones4[:], 1.0 / 256)
            nc.vector.memset(small[:, 40:41], EPS)
            dve.wait_ge(consts_in, N_CONST)
            dve.wait_ge(sig_ready, 1)
            chain(nc.vector.tensor_tensor(csil[:], csil[:], X_SG, ALU.mult))
            dve.drain().then_inc(setup_done, 1)
            for i, ph in enumerate(PHASES):
                kind, layer = ph["kind"], ph["layer"]
                if i in first_loads:
                    dve.wait_ge(layer_in, loads_until(i))
                if i == first0:
                    bias0()
                if i == first1:
                    lam1()
                if i in first23:
                    bounds(first23.index(i))
                    nc.vector.memset(AP_[:, :, 0:PAD], 0.0)
                    nc.vector.memset(AP_[:, :, PAD + S:], 0.0)
                    nc.vector.memset(ONE1, 1.0)
                    nc.vector.memset(Q2[64:P], 0.0)
                    nc.vector.memset(X[0:64, 0:6, S:T], 0.0)
                if i in att23:
                    bias2()
                if i == cond2_phase:
                    dve.wait_ge(cond2_sig, 1)
                    chain(nc.vector.tensor_tensor(csil[:, 0, :], csil[:, 0, :], ARENA[:, 15500:15500 + D], ALU.mult))
                if kind == "ada":
                    modulate(mod_share(i))
                elif kind in ("norm", "final"):
                    norm(i, ph, kind == "final")
                elif kind == "linear":
                    for n, g in enumerate(ph["groups"]):
                        if g.by in ("dve", "act+dve") or g.role.startswith("rope"):
                            take(g)
                        modulate(mod_share(i, n, len(ph["groups"])))
                        if i in mixer_phases and n >= 4:
                            if n == 4:
                                dve.drain().then_inc(dve_chain, 1)
                                chain.n += 1
                                dve.wait_ge(dve_chain, chain.n)
                            taps(range((n - 4) * 2, min((n - 3) * 2, CONV)))
                            if g.role == "z":
                                clamps(mixer_phases.index(i), g.index)
                elif kind == "attention":
                    attention(layer)
                elif kind == "conv":
                    conv(i)
                elif kind == "scan":
                    scan(i)
                end_phase(dve, i)

        @block.gpsimd
        def _(pool):
            def load(dst, src, s):
                nc.gpsimd.dma_start(dst, src).then_inc(s, 16)

            steps = [0]

            def inverse_root(dst, src):
                steps[0] += 1
                nc.gpsimd.tensor_scalar(src, src, EPS, None, ALU.add).then_inc(pool_step, 1)
                pool.wait_ge(pool_step, steps[0])
                return nc.gpsimd.tensor_tensor(dst, src, small[:, 44:44 + dst.shape[1]], ALU.pow)

            def layer_loads(i):
                if i == first0:
                    load(COS, a["cos"], layer_in)
                    load(SIN, a["sin"], layer_in)
                    load(WIN, a["win"], layer_in)
                    load(SINK, a["sink"], layer_in)
                    load(NA, a["na"], layer_in)
                    for r in range(ROWS):
                        src = bass.AP(a["rpb"].tensor, 31 * r, [[1, 16], [15 * 31, 8], [1, 265]])
                        load(RPBW[16 * r:16 * r + 16], src, layer_in)
                if i == first1:
                    load(COS, a["cos"], layer_in)
                    load(SIN, a["sin"], layer_in)
                    load(SUBG, a["subg"], layer_in)
                    load(LAMV, a["lam"], layer_in)
                if i in first23:
                    k = first23.index(i)
                    load(LEVM.bitcast(I32), a["lev"], layer_in)
                    load(CAW, a["caw"][k], layer_in)
                    load(CAV, a["cav"][k], layer_in)
                    load(GAM, a["gam"], layer_in)
                    load(RNW, a["rnw"][k], layer_in)
                if i in up23:
                    load(CFW, a["cfw"][up23.index(i)], layer_in)
                if i in att23:
                    load(BIAS[:, 0, :], a["dist"], layer_in)
                    load(BIAS[:, 1, :], a["logc"], layer_in)

            nc.gpsimd.memset(small[:, 44:48], -0.5).then_inc(pool_step, 1)
            steps[0] = 1
            pool.wait_ge(pool_step, 1)
            for i, ph in enumerate(PHASES):
                kind, layer = ph["kind"], ph["layer"]
                if i == cond2_phase:
                    load(csil[:, 0, :], a["cond"][:, 2, :], cond2_in)
                if i in first_loads:
                    layer_loads(i)
                if kind == "linear":
                    for g in ph["groups"]:
                        if g.role.startswith("rope"):
                            n = rope_groups.index(g)
                            pool.wait_ge(rot_ready, n + 1)
                            r = ROTB[:, n % 2, 0:S]
                            nc.gpsimd.tensor_tensor(r, r, SIN, ALU.mult).then_inc(rot_scaled, 1)
                        elif g.role == "relu":
                            n = relu_groups.index(g)
                            pool.wait_ge(relu_ready, n + 1)
                            hb = HID1[:, g.index, 0:g.cols]
                            nc.gpsimd.tensor_tensor(hb, hb, hb, ALU.mult).then_inc(squared, 1)
                        elif g.role == "ffn_val":
                            n = ffn_groups.index(g) // 2
                            pool.wait_ge(gelu_ready, n + 1)
                            pool.wait_ge(conv_out, 2 * n + 2)
                            nc.gpsimd.tensor_tensor(HID[:, g.index, :], GL[:, n % 2, :], UV[:, n % 2, :], ALU.mult).then_inc(hid_ready, 1)
                    if i in mixer_phases:
                        for b in range(6):
                            pool.wait_ge(log_ready, 6 * mixer_phases.index(i) + b + 1)
                            nc.gpsimd.tensor_tensor(LF[:, b, :], LF[:, b, :], LTMP[:, b, :], ALU.add)
                elif kind == "attention" and layer == 1:
                    for j in range(len(value_items(1))):
                        pool.wait_ge(o_squares, j + 1)
                        v = small[:, 24 + j % 2:25 + j % 2]
                        inverse_root(v, small[:, 20 + j % 2:21 + j % 2]).then_inc(pool_step, 1)
                        steps[0] += 1
                        pool.wait_ge(pool_step, steps[0])
                        nc.gpsimd.tensor_scalar(v, v, small[:, 28 + j % 4:29 + j % 4], P ** 0.5, ALU.mult, ALU.mult).then_inc(o_inv, 1)
                elif kind == "scan":
                    n = scan_phases.index(i)

                    def queries(u):
                        b, d = u // 2, u % 2
                        pool.wait_ge(decay_ready, 6 * n + u + 1)
                        for li, m in enumerate(LEVELS):
                            v = 42 * n + 7 * u + li
                            if v >= 8:
                                pool.wait_ge(level_ready, v - 7)
                            w = WL[:, 7 * d + li, :].rearrange("p (t b x m) -> p t x b m", t=4, x=2, m=m)[:, :, 1 - d]
                            q = QR[:, b, :].rearrange("p (t b x m) -> p t x b m", t=4, x=2, m=m)[:, :, 1 - d]
                            dst = level_queries(v).rearrange("p a (c h b m) -> p a h c b m", c=2, h=2, m=m)
                            for hx in range(2):
                                rows = slice(64 * hx, 64 * hx + 64)
                                for half in range(2):
                                    x = nc.gpsimd.tensor_tensor(dst[rows, half, hx], w[rows, 2 * half:2 * half + 2],
                                                                q[rows, 2 * half:2 * half + 2], ALU.mult)
                            x.then_inc(query_ready, 1)

                    def roots(blk, level):
                        pool.wait_ge(query_ready, level)
                        for hx in range(2):
                            hh = 2 * blk + hx
                            pool.wait_ge(sor_ready, hh + 1)
                            if hh >= 2:
                                pool.wait_ge(so_taken, hh - 1)
                            inverse_root(small[:, 36 + 16 * hx:40 + 16 * hx], small[:, 24 + 4 * hx:28 + 4 * hx]).then_inc(so_inv, 1)
                            pool.wait_ge(so_inv, hh + 1)

                    for half in (X, H):
                        spare = half[:, :, S:T].rearrange("p k (c h v) -> p k h c v", c=2, h=2)
                        nc.gpsimd.memset(spare[0:64, :, 1], 0.0)
                        nc.gpsimd.memset(spare[64:P, :, 0], 0.0).then_inc(pool_step, 1)
                        steps[0] += 1
                        pool.wait_ge(pool_step, steps[0])
                    for u in range(6):
                        queries(u)
                        if u >= 2 and u % 2 == 0:
                            roots(3 * n + u // 2 - 1, 42 * n + 7 * u + 7)
                    roots(3 * n + 2, 42 * n + 42)
                end_phase(pool, i)



def tiles(w):
    k, n = w.shape
    return np.ascontiguousarray(w.reshape(k // P, P, n // P, P).transpose(2, 1, 0, 3))


def rows(w):
    return np.ascontiguousarray(w.T).reshape(-1, P, w.shape[0])


def columns(v):
    return v.reshape(-1, P).T


def even_order():
    cols = []
    for base in (0, 768):
        for b in range(4):
            for h in (b, b + 4):
                cols += range(base + 64 * h, base + 64 * h + 64)
        cols += range(base + 512, base + 768)
    return np.array(cols)


def kernel(**inputs):
    import concourse.bacc as bacc
    from concourse.bass_utils import run_bass_kernel_spmd

    x = {k: np.asarray(v) for k, v in inputs.items()}
    arrays = {}
    arrays["xT"] = np.concatenate([x["x"][0], x["ctx"][0]], 0).T.reshape(KT, P, T)
    arrays["cond"] = np.broadcast_to(np.stack([x["c"][0], x["c_ctx"], x["c_2"][0]])[None], (P, 3, D))
    arrays["ada_b"] = np.stack([columns(b) for b in (*x["ada_b"], *x["b_ada_2"])], 1)
    arrays["norm_g"] = np.stack([np.stack([columns(g1), columns(g2)], 1)
                                 for g1, g2 in [*zip(x["norm1_g"], x["norm2_g"]), *zip(x["norm1_w_2"], x["norm2_w_2"])]], 1)
    arrays["fin_g"] = np.stack([columns(x["final_g"]), columns(x["final_norm_w_2"])], 1)
    for layer in range(2):
        arrays[f"ada{layer}"] = rows(x["ada_w"][layer])
        arrays[f"ada{layer + 2}"] = rows(x["w_ada_2"][layer])
        arrays[f"mlp1_{layer}"] = tiles(x["mlp_w1"][layer])
        arrays[f"mlp2_{layer}"] = tiles(x["mlp_w2"][layer])
        arrays[f"in{layer + 2}"] = tiles(x["w_in_2"][layer])
        arrays[f"out{layer + 2}"] = tiles(x["w_out_2"][layer])
        arrays[f"up{layer + 2}"] = tiles(x["w_up_2"][layer])
        arrays[f"down{layer + 2}"] = tiles(x["w_down_2"][layer])
    arrays["even_in"] = tiles(x["even_w_in"][0][:, even_order()])
    arrays["odd_in"] = tiles(x["odd_w_in"][0])
    arrays["out0"] = tiles(x["even_w_out"][0])
    arrays["out1"] = tiles(x["odd_w_out"][0])
    arrays["sink"] = np.broadcast_to(x["a_sink"][0][None], (P, 8))
    arrays["rpb"] = np.pad(x["b_rpb"][0][:, ::-1, ::-1].reshape(-1), (16, 32))
    arrays["subg"] = x["subln_g"][0].reshape(P, 1)
    arrays["lam"] = np.broadcast_to(np.stack([x[k][0] for k in ("lam_q1", "lam_k1", "lam_q2", "lam_k2")])[None], (P, 4, DH))
    arrays["caw"] = x["conv_a_w_2"].transpose(0, 2, 1).reshape(2, 2, P, CONV).transpose(0, 2, 1, 3)
    arrays["cav"] = np.stack([x[k].reshape(2, 2, P) for k in ("conv_a_b_2", "ln_a_w_2", "ln_a_b_2")], -1).transpose(0, 2, 1, 3)
    arrays["gam"] = x["lb_gamma_2"].reshape(2, 2, 3, P).transpose(3, 0, 1, 2)
    arrays["rnw"] = x["rec_norm_w_2"].reshape(2, 3, P).transpose(0, 2, 1)
    arrays["cfw"] = x["conv_f_w_2"].transpose(0, 2, 1).reshape(2, 2 * NB2, P, 3).transpose(0, 2, 1, 3)
    for k, v in constants().items():
        arrays[k] = v.astype(np.int32 if k == "lev" else np.float32)
    arrays = {"in_" + k: np.ascontiguousarray(v) for k, v in arrays.items()}

    nc = bacc.Bacc("TRN2", target_bir_lowering=False, num_devices=1)
    args = {k[3:]: nc.dram_tensor(k, v.shape, mybir.dt.from_np(v.dtype), kind="ExternalInput").ap() for k, v in arrays.items()}
    out = nc.dram_tensor("outT", (KT, P, S), F32, kind="ExternalOutput").ap()
    build(nc, args, out)
    got = run_bass_kernel_spmd(nc, [arrays], core_ids=[0]).results[0]["outT"]
    return np.ascontiguousarray(np.asarray(got).reshape(D, S).T).reshape(1, S, D)
```
